# Optimizing a Trainium2 kernel written in Bass

```python
import math
import jax, jax.numpy as jnp
from jax import lax
import numpy as np

D_MODEL = 1024
BATCH = 1
SEQ = 256
DEPTH = 1

CHUNK = 64
MIX_WIDTH = D_MODEL
POOL_WIDTH = D_MODEL // 2
POOL_GROUPS = 4
POOL_GROUP_DIM = POOL_WIDTH // POOL_GROUPS
POOL_WINDOWS = (2, 4, 8, 16)
GDN_WIDTH = MIX_WIDTH - POOL_WIDTH
GDN_HEADS = 4
GDN_HEAD_DIM = GDN_WIDTH // GDN_HEADS
CONV_WIDTH = 4
D_FF = 4 * D_MODEL
EPS = 1e-6
IN_WIDTH = POOL_WIDTH + 4 * GDN_WIDTH + 2 * GDN_HEADS


def rms_norm(x, w):
    xf = x.astype(jnp.float32)
    y = xf * lax.rsqrt(jnp.mean(xf * xf, axis=-1, keepdims=True) + EPS)
    return (y * w.astype(jnp.float32)).astype(x.dtype)

def l2_norm(t):
    return t * lax.rsqrt(jnp.sum(t * t, axis=-1, keepdims=True) + EPS)

def pool_mixer(u, w_pool, pool_scale):
    B, S, _ = u.shape
    uf = u.astype(jnp.float32)
    cs = jnp.cumsum(uf, axis=1)
    count = jnp.arange(1, S + 1, dtype=jnp.float32)[None, :, None]
    outs = []
    for g, w in enumerate(POOL_WINDOWS):
        sl = slice(g * POOL_GROUP_DIM, (g + 1) * POOL_GROUP_DIM)
        c = cs[..., sl]
        prev = jnp.pad(c, ((0, 0), (w, 0), (0, 0)))[:, :S]
        mean = (c - prev) / jnp.minimum(count, float(w))
        outs.append(mean - uf[..., sl])
    pooled = jnp.stack(outs, axis=2).astype(u.dtype)
    mixed = jnp.einsum('bsgc,gcd->bsgd', pooled, w_pool)
    return mixed.reshape(B, S, POOL_WIDTH) * pool_scale

def causal_conv_silu(x, w):
    C = x.shape[-1]
    y = lax.conv_general_dilated(x, w[:, None, :].astype(x.dtype), window_strides=(1,),
                                 padding=[(CONV_WIDTH - 1, 0)],
                                 dimension_numbers=('NWC', 'WIO', 'NWC'),
                                 feature_group_count=C)
    return jax.nn.silu(y)

def gated_delta_net(q, k, v, z, a, b, a_log, dt_bias, gdn_norm):
    B, S, _ = q.shape
    H, Dh, C = GDN_HEADS, GDN_HEAD_DIM, CHUNK
    N = S // C
    f32 = jnp.float32

    def heads(t):
        return t.astype(f32).reshape(B, N, C, H, Dh).transpose(0, 3, 1, 2, 4)

    def per_head(t):
        return t.reshape(B, N, C, H).transpose(0, 3, 1, 2)

    qh = l2_norm(heads(q)) * (Dh ** -0.5)
    kh = l2_norm(heads(k))
    vh = heads(v)
    beta = per_head(jax.nn.sigmoid(b.astype(f32)))
    g = -jnp.exp(a_log.astype(f32)) * jax.nn.softplus(a.astype(f32) + dt_bias.astype(f32))
    gcum = jnp.cumsum(per_head(g), axis=-1)

    idx = jnp.arange(C)
    incl = idx[:, None] >= idx[None, :]
    strict = idx[:, None] > idx[None, :]
    diff = gcum[..., :, None] - gcum[..., None, :]
    decay_incl = jnp.exp(jnp.where(incl, diff, -jnp.inf))
    decay_strict = jnp.where(strict, decay_incl, 0.0)

    kb = kh * beta[..., None]
    m = jnp.einsum('bhncd,bhnjd->bhncj', kb, kh) * decay_strict
    lhs = jnp.eye(C, dtype=f32) + m
    rhs = jnp.concatenate([vh * beta[..., None], kb * jnp.exp(gcum)[..., None]], axis=-1)
    sol = lax.linalg.triangular_solve(lhs, rhs, left_side=True, lower=True)
    value, k_cumdecay = sol[..., :Dh], sol[..., Dh:]
    attn_inner = jnp.einsum('bhncd,bhnjd->bhncj', qh, kh) * decay_incl
    q_dec = qh * jnp.exp(gcum)[..., None]
    g_last = gcum[..., -1]
    k_dec = kh * jnp.exp(g_last[..., None] - gcum)[..., None]

    def step(state, inp):
        qd, kc, val, ai, kd, gl = inp
        v_new = val - jnp.einsum('bhcd,bhde->bhce', kc, state)
        o = jnp.einsum('bhcd,bhde->bhce', qd, state) + jnp.einsum('bhcj,bhje->bhce', ai, v_new)
        state = state * jnp.exp(gl)[..., None, None] + jnp.einsum('bhcd,bhce->bhde', kd, v_new)
        return state, o

    xs = (jnp.moveaxis(q_dec, 2, 0), jnp.moveaxis(k_cumdecay, 2, 0), jnp.moveaxis(value, 2, 0),
          jnp.moveaxis(attn_inner, 2, 0), jnp.moveaxis(k_dec, 2, 0), jnp.moveaxis(g_last, 2, 0))
    state0 = jnp.zeros((B, H, Dh, Dh), f32)
    _, o = lax.scan(step, state0, xs)
    o = o.transpose(1, 0, 3, 2, 4).reshape(B, S, H, Dh)
    o = o * lax.rsqrt(jnp.mean(o * o, axis=-1, keepdims=True) + EPS) * gdn_norm.astype(f32)
    o = o * jax.nn.silu(z.astype(f32).reshape(B, S, H, Dh))
    return o.reshape(B, S, GDN_WIDTH).astype(q.dtype)

def first_inputs(seed: int = 0) -> dict:
    key = jax.random.key(seed)
    ks = jax.random.split(key, 16)
    nrm = jax.random.normal
    H, Dh = GDN_HEADS, GDN_HEAD_DIM
    x = nrm(ks[0], (BATCH, SEQ, D_MODEL), jnp.float32)
    norm_mix = 1.0 + 0.02 * nrm(ks[1], (DEPTH, D_MODEL), jnp.float32)
    w_in = nrm(ks[2], (DEPTH, D_MODEL, IN_WIDTH), jnp.float32) * D_MODEL ** -0.5
    conv_w = nrm(ks[3], (DEPTH, CONV_WIDTH, 3 * GDN_WIDTH), jnp.float32) * CONV_WIDTH ** -0.5
    w_pool = nrm(ks[4], (DEPTH, POOL_GROUPS, POOL_GROUP_DIM, POOL_GROUP_DIM), jnp.float32) * POOL_GROUP_DIM ** -0.5
    pool_scale = 1.0 + 0.1 * nrm(ks[5], (DEPTH, POOL_WIDTH), jnp.float32)
    a_log = jnp.log(jax.random.uniform(ks[6], (DEPTH, H), jnp.float32, 1.0, 16.0))
    dt = jnp.exp(jax.random.uniform(ks[7], (DEPTH, H), jnp.float32, math.log(1e-3), math.log(1e-1)))
    dt_bias = dt + jnp.log(-jnp.expm1(-dt))
    gdn_norm = 1.0 + 0.02 * nrm(ks[8], (DEPTH, Dh), jnp.float32)
    w_out = nrm(ks[9], (DEPTH, MIX_WIDTH, D_MODEL), jnp.float32) * MIX_WIDTH ** -0.5
    norm_mlp = 1.0 + 0.02 * nrm(ks[10], (DEPTH, D_MODEL), jnp.float32)
    w_up = nrm(ks[11], (DEPTH, D_MODEL, D_FF), jnp.float32) * D_MODEL ** -0.5
    w_down = nrm(ks[12], (DEPTH, D_FF, D_MODEL), jnp.float32) * D_FF ** -0.5
    norm_final = 1.0 + 0.02 * nrm(ks[13], (D_MODEL,), jnp.float32)
    return {"x": x, "norm_mix": norm_mix, "w_in": w_in, "conv_w": conv_w, "w_pool": w_pool,
            "pool_scale": pool_scale, "a_log": a_log, "dt_bias": dt_bias, "gdn_norm": gdn_norm,
            "w_out": w_out, "norm_mlp": norm_mlp, "w_up": w_up, "w_down": w_down,
            "norm_final": norm_final}

def first_block(x, norm_mix, w_in, conv_w, w_pool, pool_scale, a_log, dt_bias, gdn_norm,
              w_out, norm_mlp, w_up, w_down, norm_final):
    P, G, H = POOL_WIDTH, GDN_WIDTH, GDN_HEADS
    h = x
    for l in range(DEPTH):
        u = rms_norm(h, norm_mix[l])
        proj = u @ w_in[l]
        pool_out = pool_mixer(proj[..., :P], w_pool[l], pool_scale[l])
        qkv = causal_conv_silu(proj[..., P:P + 3 * G], conv_w[l])
        z = proj[..., P + 3 * G:P + 4 * G]
        a = proj[..., P + 4 * G:P + 4 * G + H]
        b = proj[..., P + 4 * G + H:P + 4 * G + 2 * H]
        gdn_out = gated_delta_net(qkv[..., :G], qkv[..., G:2 * G], qkv[..., 2 * G:], z, a, b,
                                  a_log[l], dt_bias[l], gdn_norm[l])
        mix = jnp.concatenate([pool_out, gdn_out], axis=-1)
        h = h + mix @ w_out[l]
        u = rms_norm(h, norm_mlp[l])
        h = h + jnp.square(jax.nn.relu(u @ w_up[l])) @ w_down[l]
    return rms_norm(h, norm_final)


DEPTH_2 = 2

N_MIXERS = 2
N_LAYERS_A = (DEPTH_2 + 1) // 2
N_LAYERS_B = DEPTH_2 // 2
SGU_BLOCK = 128
SGU_WIDTH = 2 * D_MODEL
SGU_GROUPS = 16
SGU_GROUP_DIM = SGU_WIDTH // SGU_GROUPS
RWKV_HEAD_DIM = 64
RWKV_HEADS = D_MODEL // RWKV_HEAD_DIM
DECAY_LORA = 64
AAA_LORA = 64
MV_LORA = 32
GATE_LORA = 128
FFN_HIDDEN = 4 * D_MODEL
RMS_EPS = 1e-6
LN_EPS = 1e-5
GN_EPS = 64e-5


def _rmsnorm(x, g):
    xf = x.astype(jnp.float32)
    y = xf * lax.rsqrt(jnp.mean(xf * xf, axis=-1, keepdims=True) + RMS_EPS)
    return (y * g.astype(jnp.float32)).astype(x.dtype)

def _layernorm(x, g, b, eps):
    xf = x.astype(jnp.float32)
    mu = jnp.mean(xf, axis=-1, keepdims=True)
    var = jnp.mean(jnp.square(xf - mu), axis=-1, keepdims=True)
    y = (xf - mu) * lax.rsqrt(var + eps)
    return (y * g.astype(jnp.float32) + b.astype(jnp.float32)).astype(x.dtype)

def _sgu_mask():
    chunk_id = jnp.arange(SGU_BLOCK) // CHUNK
    return chunk_id[None, :] <= chunk_id[:, None]

def _spatial_gating_mixer(h, w_in, b_in, ln_g, ln_b, w_s, b_s, w_out):
    bsz, seq, _ = h.shape
    z = jax.nn.gelu(h @ w_in + b_in, approximate=False)
    u, v = jnp.split(z, 2, axis=-1)
    v = _layernorm(v, ln_g, ln_b, LN_EPS)
    v = v.reshape(bsz, seq // SGU_BLOCK, SGU_BLOCK, SGU_GROUPS, SGU_GROUP_DIM)
    w_s = w_s * _sgu_mask()[None].astype(w_s.dtype)
    s = jnp.einsum('gij,bnjgc->bnigc', w_s, v) + b_s.T[None, None, :, :, None]
    y = u * s.reshape(bsz, seq, SGU_WIDTH)
    return y @ w_out

def _wkv7_scan(r, w, k, v, kk, kka):
    bsz, _, nh, n = r.shape
    xs = tuple(jnp.moveaxis(t, 1, 0) for t in (r, w, k, v, kk, kka))

    def step(S, inp):
        r_t, w_t, k_t, v_t, kk_t, kka_t = inp
        sa = jnp.einsum('bhvk,bhk->bhv', S, -kk_t)
        S = (S * w_t[:, :, None, :] + sa[..., None] * kka_t[:, :, None, :]
             + v_t[..., None] * k_t[:, :, None, :])
        y = jnp.einsum('bhvk,bhk->bhv', S, r_t)
        return S, y

    S0 = jnp.zeros((bsz, nh, n, n), jnp.float32)
    _, y = lax.scan(step, S0, xs)
    return jnp.moveaxis(y, 0, 1)

def _rwkv7_mixer(h, mu, w_rkv, w0, w_la, w_lb, a0, a_la, a_lb, g_la, g_lb,
                 k_k, k_a, r_k, ln_g, ln_b, w_o, v_first, v_mix):
    bsz, seq, d = h.shape
    f32 = jnp.float32

    def heads(t):
        return t.reshape(bsz, seq, RWKV_HEADS, RWKV_HEAD_DIM)

    xx = jnp.pad(h, ((0, 0), (1, 0), (0, 0)))[:, :-1] - h
    xs = h[None] + xx[None] * mu[:, None, None, :]
    rkv = jnp.einsum('pbtd,pde->pbte', xs[:3], w_rkv)
    r, k, v = rkv[0], rkv[1], rkv[2]
    xv, xw, xa, xg = xs[2], xs[3], xs[4], xs[5]
    log_w = -jax.nn.softplus(-(w0 + jnp.tanh(xw @ w_la) @ w_lb)) - 0.5
    decay = jnp.exp(-jnp.exp(log_w.astype(f32)))
    if v_mix is None:
        v_first = v
    else:
        v0, v_la, v_lb = v_mix
        v = v + (v_first - v) * jax.nn.sigmoid(v0 + (xv @ v_la) @ v_lb)
    a = jax.nn.sigmoid(a0 + (xa @ a_la) @ a_lb)
    g = jax.nn.sigmoid(xg @ g_la) @ g_lb
    kk = heads(k * k_k).astype(f32)
    kk = kk / jnp.maximum(jnp.sqrt(jnp.sum(kk * kk, axis=-1, keepdims=True)), 1e-12)
    k = k * (1.0 + (a - 1.0) * k_a)
    r_h, k_h, v_h = heads(r).astype(f32), heads(k).astype(f32), heads(v).astype(f32)
    y = _wkv7_scan(r_h, heads(decay), k_h, v_h, kk, kk * heads(a).astype(f32))
    mu_y = jnp.mean(y, axis=-1, keepdims=True)
    var_y = jnp.mean(jnp.square(y - mu_y), axis=-1, keepdims=True)
    y = ((y - mu_y) * lax.rsqrt(var_y + GN_EPS)).reshape(bsz, seq, d)
    y = y * ln_g.astype(f32) + ln_b.astype(f32)
    bonus = jnp.sum(r_h * k_h * r_k.astype(f32), axis=-1, keepdims=True) * v_h
    y = (y + bonus.reshape(bsz, seq, d)) * g.astype(f32)
    return y.astype(h.dtype) @ w_o, v_first

def _squared_relu_mlp(h, w1, w2):
    return jnp.square(jax.nn.relu(h @ w1)) @ w2

def second_inputs(seed: int = 0) -> dict:
    key = jax.random.key(seed)
    ks = jax.random.split(key, 32)
    f32 = jnp.float32
    D, E, G, H, N = D_MODEL, SGU_WIDTH, SGU_GROUPS, RWKV_HEADS, RWKV_HEAD_DIM
    nA, nB = N_LAYERS_A, N_LAYERS_B

    def nrm(k, shape, scale):
        return jax.random.normal(k, shape, f32) * scale

    return {
        "x": nrm(ks[0], (BATCH, SEQ, D), 1.0),
        "norm_mix_g": 1.0 + nrm(ks[1], (DEPTH_2, D), 0.05),
        "norm_ffn_g": 1.0 + nrm(ks[2], (DEPTH_2, D), 0.05),
        "final_norm_g": 1.0 + nrm(ks[3], (D,), 0.05),
        "ffn_w1": nrm(ks[4], (DEPTH_2, D, FFN_HIDDEN), D ** -0.5),
        "ffn_w2": nrm(ks[5], (DEPTH_2, FFN_HIDDEN, D), 0.5 * FFN_HIDDEN ** -0.5),
        "sgu_w_in": nrm(ks[6], (nA, D, 2 * E), D ** -0.5),
        "sgu_b_in": nrm(ks[7], (nA, 2 * E), 0.02),
        "sgu_ln_g": 1.0 + nrm(ks[8], (nA, E), 0.05),
        "sgu_ln_b": nrm(ks[9], (nA, E), 0.02),
        "sgu_w_s": nrm(ks[10], (nA, G, SGU_BLOCK, SGU_BLOCK), SGU_BLOCK ** -0.5),
        "sgu_b_s": 1.0 + nrm(ks[11], (nA, G, SGU_BLOCK), 0.1),
        "sgu_w_out": nrm(ks[12], (nA, E, D), 0.5 * E ** -0.5),
        "rwkv_mu": jax.random.uniform(ks[13], (nB, 6, D), f32),
        "rwkv_w_rkv": nrm(ks[14], (nB, 3, D, D), D ** -0.5),
        "rwkv_w0": jax.random.uniform(ks[15], (nB, D), f32, -6.0, 0.5),
        "rwkv_w_lora_a": nrm(ks[16], (nB, D, DECAY_LORA), D ** -0.5),
        "rwkv_w_lora_b": nrm(ks[17], (nB, DECAY_LORA, D), 0.3 * DECAY_LORA ** -0.5),
        "rwkv_a0": nrm(ks[18], (nB, D), 0.1),
        "rwkv_a_lora_a": nrm(ks[19], (nB, D, AAA_LORA), D ** -0.5),
        "rwkv_a_lora_b": nrm(ks[20], (nB, AAA_LORA, D), 0.3 * AAA_LORA ** -0.5),
        "rwkv_v0": 0.5 + nrm(ks[21], (nB - 1, D), 0.1),
        "rwkv_v_lora_a": nrm(ks[22], (nB - 1, D, MV_LORA), D ** -0.5),
        "rwkv_v_lora_b": nrm(ks[23], (nB - 1, MV_LORA, D), 0.3 * MV_LORA ** -0.5),
        "rwkv_g_lora_a": nrm(ks[24], (nB, D, GATE_LORA), D ** -0.5),
        "rwkv_g_lora_b": nrm(ks[25], (nB, GATE_LORA, D), GATE_LORA ** -0.5),
        "rwkv_k_k": 0.85 + nrm(ks[26], (nB, D), 0.05),
        "rwkv_k_a": 1.0 + nrm(ks[27], (nB, D), 0.05),
        "rwkv_r_k": nrm(ks[28], (nB, H, N), 0.1),
        "rwkv_ln_g": 1.0 + nrm(ks[29], (nB, D), 0.05),
        "rwkv_ln_b": nrm(ks[30], (nB, D), 0.02),
        "rwkv_w_o": nrm(ks[31], (nB, D, D), 0.5 * D ** -0.5),
    }

def second_block(x, norm_mix_g, norm_ffn_g, final_norm_g, ffn_w1, ffn_w2,
              sgu_w_in, sgu_b_in, sgu_ln_g, sgu_ln_b, sgu_w_s, sgu_b_s, sgu_w_out,
              rwkv_mu, rwkv_w_rkv, rwkv_w0, rwkv_w_lora_a, rwkv_w_lora_b,
              rwkv_a0, rwkv_a_lora_a, rwkv_a_lora_b,
              rwkv_v0, rwkv_v_lora_a, rwkv_v_lora_b,
              rwkv_g_lora_a, rwkv_g_lora_b, rwkv_k_k, rwkv_k_a, rwkv_r_k,
              rwkv_ln_g, rwkv_ln_b, rwkv_w_o):
    v_first = None
    for i in range(DEPTH_2):
        h = _rmsnorm(x, norm_mix_g[i])
        j = i // N_MIXERS
        if i % N_MIXERS == 0:
            y = _spatial_gating_mixer(h, sgu_w_in[j], sgu_b_in[j], sgu_ln_g[j], sgu_ln_b[j],
                                      sgu_w_s[j], sgu_b_s[j], sgu_w_out[j])
        else:
            v_mix = None if j == 0 else (rwkv_v0[j - 1], rwkv_v_lora_a[j - 1], rwkv_v_lora_b[j - 1])
            y, v_first = _rwkv7_mixer(h, rwkv_mu[j], rwkv_w_rkv[j], rwkv_w0[j],
                                      rwkv_w_lora_a[j], rwkv_w_lora_b[j],
                                      rwkv_a0[j], rwkv_a_lora_a[j], rwkv_a_lora_b[j],
                                      rwkv_g_lora_a[j], rwkv_g_lora_b[j],
                                      rwkv_k_k[j], rwkv_k_a[j], rwkv_r_k[j],
                                      rwkv_ln_g[j], rwkv_ln_b[j], rwkv_w_o[j],
                                      v_first, v_mix)
        x = x + y
        x = x + _squared_relu_mlp(_rmsnorm(x, norm_ffn_g[i]), ffn_w1[i], ffn_w2[i])
    return _rmsnorm(x, final_norm_g)


def setup_inputs(seed=0):
    out = dict(first_inputs(seed))
    for name, value in second_inputs(seed + 1).items():
        if name != "x":
            out[name + "_2"] = value
    return out


def reference(
    x, norm_mix, w_in, conv_w, w_pool, pool_scale, a_log, dt_bias, gdn_norm, w_out, norm_mlp,
    w_up, w_down, norm_final, norm_mix_g_2, norm_ffn_g_2, final_norm_g_2, ffn_w1_2, ffn_w2_2,
    sgu_w_in_2, sgu_b_in_2, sgu_ln_g_2, sgu_ln_b_2, sgu_w_s_2, sgu_b_s_2, sgu_w_out_2,
    rwkv_mu_2, rwkv_w_rkv_2, rwkv_w0_2, rwkv_w_lora_a_2, rwkv_w_lora_b_2, rwkv_a0_2,
    rwkv_a_lora_a_2, rwkv_a_lora_b_2, rwkv_v0_2, rwkv_v_lora_a_2, rwkv_v_lora_b_2,
    rwkv_g_lora_a_2, rwkv_g_lora_b_2, rwkv_k_k_2, rwkv_k_a_2, rwkv_r_k_2, rwkv_ln_g_2,
    rwkv_ln_b_2, rwkv_w_o_2,
):
    x = first_block(
        x, norm_mix, w_in, conv_w, w_pool, pool_scale, a_log, dt_bias, gdn_norm, w_out,
        norm_mlp, w_up, w_down, norm_final,
    )
    return second_block(
        x, norm_mix_g_2, norm_ffn_g_2, final_norm_g_2, ffn_w1_2, ffn_w2_2, sgu_w_in_2,
        sgu_b_in_2, sgu_ln_g_2, sgu_ln_b_2, sgu_w_s_2, sgu_b_s_2, sgu_w_out_2, rwkv_mu_2,
        rwkv_w_rkv_2, rwkv_w0_2, rwkv_w_lora_a_2, rwkv_w_lora_b_2, rwkv_a0_2, rwkv_a_lora_a_2,
        rwkv_a_lora_b_2, rwkv_v0_2, rwkv_v_lora_a_2, rwkv_v_lora_b_2, rwkv_g_lora_a_2,
        rwkv_g_lora_b_2, rwkv_k_k_2, rwkv_k_a_2, rwkv_r_k_2, rwkv_ln_g_2, rwkv_ln_b_2,
        rwkv_w_o_2,
    )


_drawn_inputs = setup_inputs


def setup_inputs(seed=0):
    import zlib

    import numpy as np

    out = dict(_drawn_inputs(seed))
    spreads = {}
    factors = {'norm_mix': 2.822,
     'gdn_norm': 6.502,
     'norm_mlp': 3.088,
     'sgu_b_in_2': 4.931,
     'sgu_ln_g_2': 3.876,
     'sgu_ln_b_2': 8.0,
     'rwkv_w_lora_a_2': 8.0,
     'rwkv_w_lora_b_2': 8.0,
     'rwkv_a0_2': 5.141,
     'rwkv_ln_g_2': 5.074,
     'rwkv_ln_b_2': 8.0}
    for name, (base, spread) in spreads.items():
        noise = np.random.default_rng([zlib.crc32(name.encode()), seed]).standard_normal(out[name].shape)
        drawn = base * np.exp(spread * noise) if base else spread * noise
        out[name] = __import__('jax').numpy.asarray(drawn.astype(out[name].dtype))
    for name, factor in factors.items():
        out[name] = (out[name] * factor).astype(out[name].dtype)
    return out
```

```python
from contextlib import ExitStack

import concourse.bass as bass
import numpy as np
from concourse import mybir

F32 = mybir.dt.float32
F32R = mybir.dt.float32r
ALU = mybir.AluOpType
ACT = mybir.ActivationFunctionType
AX_X = mybir.AxisListType.X

P = 128
T = 256
D = 1024
KT = D // P
CH = T // P
EPS = 1e-6
FF = 4 * D
FCH = FF // 512

IN_WIDTH = 2568
NPOOL, NGDN = 4, 4
CONV = 4
SGU_E = 2048
GT = SGU_E // P
RH, RN = 16, 64
LN_EPS = 1e-5
GN_EPS = 64e-5

UNIT = 2048
RING = 4
U_IN = 0
U_OUT = U_IN + 10
U_FFN1 = U_OUT + 4
U_SGU = U_FFN1 + 4 * FCH
U_SGO = U_SGU + 16
U_FFN2 = U_SGO + 8
U_LORA = U_FFN2 + 4 * FCH
U_RKV = U_LORA + 1
U_WO = U_RKV + 12
U_FFN3 = U_WO + 4
U_END = U_FFN3 + 4 * FCH

VECS = {}
_at = 0
for _name, _n in [
    ("norm_mix", 8), ("conv_w", 48), ("pool_scale", 4), ("gdn_norm", 1), ("norm_mlp", 8),
    ("norm_final", 8), ("norm_mix_g0", 8), ("norm_ffn_g0", 8), ("norm_mix_g1", 8),
    ("norm_ffn_g1", 8), ("final_norm_g", 8), ("b_in_u", 16), ("sgu_ln_g", 16), ("sgu_ln_b", 16),
    ("mu", 48), ("a0", 8), ("k_k", 8), ("k_a", 8), ("r_k", 8), ("rwkv_ln_g", 8),
    ("rwkv_ln_b", 8), ("a_log", 4), ("dt_bias", 4),
]:
    VECS[_name] = (_at, _n)
    _at += _n
NV = _at

LEVELS = 7
CMATS = {}
_at = 0
for _name, _n in [
    ("ident", P), ("upper", P), ("upper_strict", P), ("neg_upper_strict", P), ("lower_strict", P),
    ("levels", LEVELS * P), ("cum", P + 1), ("heads", P), ("pool_head", 64), ("ones", P),
]:
    CMATS[_name] = (_at, _n)
    _at += _n
NCM = _at


def constant_matrices():
    i = np.arange(P)[:, None]
    j = np.arange(P)[None, :]
    m = {
        "ident": i == j, "upper": i <= j, "upper_strict": i < j,
        "neg_upper_strict": -1.0 * (i < j), "lower_strict": i > j,
        "levels": np.concatenate(
            [(i // (2 * b) == j // (2 * b)) & (i % (2 * b) < b) & (j % (2 * b) >= b)
             for b in (1 << l for l in range(LEVELS))], 1),
        "cum": 1.0 * (i <= np.arange(-1, P)[None, :]) - 1.0 * (i <= P // 2 - 1),
        "heads": i // RN == j // RN,
        "pool_head": np.broadcast_to(np.concatenate(
            [1.0 / np.minimum(np.arange(1, 17), 2.0 ** (g + 1)) for g in range(NPOOL)])[None], (P, 64)),
        "ones": np.ones((P, P)),
    }
    return np.concatenate([np.asarray(m[n], np.float32) for n in CMATS], 1)


class Buffers:
    pass


class Chain:

    def __init__(self, engine, semaphore):
        self.engine, self.semaphore, self.n = engine, semaphore, 0

    def add(self, instruction):
        instruction.then_inc(self.semaphore, 1)
        self.n += 1
        return self.n

    def settle(self, n=None):
        self.engine.wait_ge(self.semaphore, self.n if n is None else n)


def build_program(nc, dram, out, last_phase="end"):
    with ExitStack() as ctx:
        build_on(ctx, nc, dram, out, last_phase)


def build_on(ctx, nc, dram, out, last_phase):
    def sb(name, shape, dtype=F32):
        return ctx.enter_context(nc.sbuf_tensor("sb_" + name, shape, dtype))

    def sem(name):
        return ctx.enter_context(nc.semaphore(name))

    PHASES = ["mixer", "ffn1", "sgu", "ffn2", "rwkv", "end"]
    on = {p: PHASES.index(p) <= PHASES.index(last_phase) for p in PHASES}
    n_units = {"mixer": U_FFN1, "ffn1": U_SGU, "sgu": U_FFN2, "ffn2": U_LORA, "rwkv": U_FFN3,
               "end": U_END}[last_phase]

    raw = [sb(f"raw{s}", [P, UNIT]) for s in range(RING)]
    whi = [sb(f"w_high{s}", [P, UNIT], F32R) for s in range(RING)]
    wlo = [sb(f"w_low{s}", [P, UNIT], F32R) for s in range(RING)]
    x = sb("x", [P, KT, T])
    vec = sb("vectors", [P, NV])
    cm = sb("constants", [P, NCM])
    shared = sb("shared", [P, 3 * UNIT])
    at = nc.sbuf_base - 3 * UNIT * 4

    def place(name, offset, shape, dtype=F32):
        return nc.alloc_sbuf_tensor_at("sb_" + name, shape, dtype, offset=at + 4 * offset)

    act_hi = place("act_high", 0, [P, KT, T], F32R)
    act_lo = place("act_low", UNIT, [P, KT, T], F32R)
    hid_hi = place("hidden_high", 2 * UNIT, [P, 4, T], F32R)
    hid_lo = place("hidden_low", 2 * UNIT + 4 * T, [P, 4, T], F32R)
    over_act = place("over_act", 0, [P, 2 * UNIT])
    over_hid = place("over_hidden", 2 * UNIT, [P, UNIT])
    ARENA = 16896
    arena = sb("arena", [P, ARENA])
    bank = [ctx.enter_context(nc.psum_tensor(f"bank{b}", [P, 512], F32)) for b in range(8)]

    def carve(start, *shape):
        n = int(np.prod(shape))
        assert start + n <= ARENA, (start, n, ARENA)
        v = arena[:, start:start + n]
        if len(shape) == 2:
            v = v.rearrange("p (a b) -> p a b", b=shape[1])
        elif len(shape) == 3:
            v = v.rearrange("p (a b c) -> p a b c", b=shape[1], c=shape[2])
        return v

    def vcol(name, k=0, n=1):
        a = VECS[name][0]
        return vec[:, a + k:a + k + n]

    def cmat(name, k=0):
        a, n = CMATS[name]
        return cm[:, a + k * P:a + k * P + min(P, n)]

    def tap_weight(t, tap):
        wt = {0: 4, 1: 0, 2: 8}[t // 4] + t % 4
        return vcol("conv_w", 4 * wt + 3 - tap)

    ident, ones = cmat("ident"), cmat("ones")
    f32 = lambda ap: ap.bitcast(F32)
    two = lambda ap: ap.rearrange("p (a b) -> p a b", a=2)

    def over(ap, n):
        return ap.rearrange("p (a b) -> p a b", a=1).broadcast_to([P, n, ap.shape[1]])

    landed = [sem(f"unit_landed{s}") for s in range(RING)]
    hi_done = sem("unit_high")
    lo_done = sem("unit_low")
    w_used = sem("unit_used")

    def landed_value(u):
        n = u // RING + 1
        if u >= U_LORA and u % RING == U_LORA % RING:
            n += 2
        return 16 * n

    act_chain, dve_chain, pool_chain = sem("act_chain"), sem("dve_chain"), sem("pool_chain")

    vec_in, x_in, cm_in, ab_in, wpool_in = (sem(n) for n in (
        "vectors_in", "x_in", "constants_in", "ab_weights_in", "pool_weights_in"))
    a_hi = sem("activation_high")
    a_lo = sem("activation_low")
    A_MIX, A_OUT, A_FFN1, A_SGU, A_FFN2, A_RWKV = 0, 8, 16, 24, 32, 40
    A_WO, A_FFN3 = A_RWKV + 48, A_RWKV + 56
    sq_done = sem("squares")
    ss_done = sem("square_sums")
    r_done = sem("scales")
    x_done = sem("residual")
    X_MIX, X_FFN1, X_FIN, X_SGU, X_FFN2, X_RWKV, X_FFN3 = 0, 4, 8, 12, 16, 20, 24

    proj_out = sem("proj_taken")
    ab_ps, ab_col, rtok_ps = sem("ab_in_psum"), sem("gates_by_token"), sem("token_scales_in_psum")
    g_ready, gsum_ps, decay_done = sem("log_decays"), sem("decay_sums_in_psum"), sem("decays")
    decay_mask = sem("masked_decays")
    conv_first, conv_done, silu_done = sem("first_tap"), sem("convolved"), sem("activated")
    box_sum = sem("trailing_sums")
    kqn_done, prod_ps = sem("keys_queries_normalised"), sem("products_in_psum")
    tr_ps, tr_done = sem("transposed_in_psum"), sem("transposed")
    pool_sum, pool_ps = sem("pooled"), sem("pool_mixed_in_psum")
    step_ps, step_sb = sem("step_in_psum"), sem("step_taken")
    z_done = sem("gate_z")
    lt_ready = sem("l_transposed")
    inv_lt, inv_x_ps, inv_x, inv_d_ps = (sem(n) for n in (
        "inv_level", "inv_x_psum", "inv_x", "inv_d_psum"))
    inv_wt, inv_t_ps, inv_w = sem("inv_wt"), sem("inv_t_psum"), sem("inv_w")
    up_ps, relu_done, h_hi, h_lo = sem("up_in_psum"), sem("relu"), sem("hidden_hi"), sem("hidden_lo")
    acc_ps = sem("accumulated")
    stored = sem("stored")

    MX = Buffers()
    c = 0
    MX.pre = carve(c, 12, T + 3)
    MX.WT, MX.W, MX.X = carve(c, 8, P), carve(c + 1024, 8, P), carve(c + 2048, 8, P)
    MX.pu = carve(c + 1024, 4, T + 16)
    MX.mix = carve(c + 1024 + 4 * (T + 16), 4, T)
    c += 1024 + 4 * (T + 16) + 4 * T
    MX.qkv = carve(c, 12, T)
    c += 12 * T
    MX.z = carve(c, 4, T)
    c += 4 * T
    MX.ET, MX.R = carve(c, 8, P), carve(c, 8, P)
    c += 1024
    MX.AT = carve(c, 8, P)
    c += 1024
    MX.LT = carve(c, 8, P)
    MX.GS = carve(c, 8, P)
    c += 1024
    MX.sq = carve(c, KT, T)
    MX.LTl = carve(c, 8, P)
    MX.rko = carve(c + 1024, 4, T)
    MX.box = MX.rko
    c += 2048
    MX.Vt, MX.vn = carve(c, 8, P), carve(c + 1024, 8, P)
    MX.GO = carve(c + 1024, 4, P)
    MX.doubling = [carve(c + 1024 + (T + 16) * i, T + 16) for i in range(2)]
    c += 2048
    MX.Kd, MX.S, MX.qg = carve(c, 4, P), carve(c + 512, 4, P), carve(c + 1024, 4, P)
    c += 1536
    MX.rB = carve(c, T)
    c += T
    MX.wpool = carve(c, 4, P)
    c += 512
    MX.wab = carve(c, KT, 8)
    c += 64
    MX.ab = carve(c, CH, 8)
    c += 16
    MX.s = [carve(c + 8 * i, CH, 4) for i in range(12)]
    c += 96
    epst = sb("epsilons", [P, 4])
    wab_hi, wab_lo = sb("ab_high", [P, KT, 8], F32R), sb("ab_low", [P, KT, 8], F32R)

    def by_k(w):
        return w.rearrange("(k p) n -> p k n", p=P)

    w_in_v, w_out_v, sgu_in_v = by_k(dram["w_in"][0]), by_k(dram["w_out"][0]), by_k(dram["sgu_w_in_2"][0])
    sgu_out_v, wo_v = by_k(dram["sgu_w_out_2"][0]), by_k(dram["rwkv_w_o_2"][0])
    rkv_v = [by_k(dram["rwkv_w_rkv_2"][0, i]) for i in range(3)]
    ffn_v = [(by_k(dram["w_up"][0]), by_k(dram["w_down"][0])),
             (by_k(dram["ffn_w1_2"][0]), by_k(dram["ffn_w2_2"][0])),
             (by_k(dram["ffn_w1_2"][1]), by_k(dram["ffn_w2_2"][1]))]
    FFN_U = [U_FFN1, U_FFN2, U_FFN3]
    IN_COLS = [4, 5, 2, 3, 6, 7, 0, 1, 8, 9]

    FB = Buffers()
    FB.r, FB.h = carve(0, 4, T), carve(1024, 4, T)
    FB.sq = carve(2048, KT, T)
    FB.r2 = carve(14336, T)
    FB.t = [carve(14848 + 512 * i, 2, T) for i in range(2)]
    SG = Buffers()
    SG.V = carve(0, CH, SGU_E)
    SG.h = carve(0, KT, T)
    SG.U = carve(4096, GT, T)
    SG.sq = [carve(4096, KT, T), carve(6144, KT, T)]
    SG.ws = carve(8192, GT, P)
    SG.bv = carve(10240, SGU_E)
    SG.T = carve(12288, GT, P)
    SG.r = [carve(14336 + T * i, T) for i in range(2)]
    SG.y = [carve(14848 + 512 * i, 2, T) for i in range(2)]
    SG.stats = carve(15872, CH, 4, 6)
    SG.mv = carve(15920, CH, 2)
    SG.rs = carve(15924, CH, 1)
    zeros = sb("zeros", [P, T], F32R)

    sgu_in = sem("gating_parameters_in")
    every = lambda row: row.broadcast_to([P, row.shape[1]])
    r_sq = sem("relu_squared")
    v_raw, v_act, v_stat, u_act, vn_done = (sem(n) for n in (
        "v_in", "v_activated", "v_statistics", "u_activated", "v_normalised"))
    y_done, sp_ps, t_done = sem("gated"), sem("spatial_in_psum"), sem("spatial_shift")
    mask_done, rs_ps, norm_done = sem("spatial_masked"), sem("spatial_row_sums"), sem("normalised")
    zero_done = sem("zeros_ready")

    FFN_A = [A_FFN1, A_FFN2, A_FFN3]
    FFN_X = [X_MIX, X_SGU, X_RWKV]
    FFN_XO = [X_FFN1, X_FFN2, X_FFN3]
    FFN_G = ["norm_mlp", "norm_ffn_g0", "norm_ffn_g1"]
    FFN_H = [0, 24, 40]
    H_SGU = 16
    FFN_ACC = [0, 6, 9]
    ACC_SGU = 3
    SS = {"mixer": 0, "ffn1": 7, "sgu": 8, "ffn2": 10, "rwkv": 11, "ffn3": 12, "final": 13}
    SQ = {"mixer": 0, "ffn1": 7, "sgu": 8, "ffn2": 16, "rwkv": 17, "ffn3": 21, "final": 22}
    RD = {"sgu": 7, "rwkv": 9, "final": 10}

    RW = Buffers()
    RW.H = carve(0, KT, T + 1)
    RW.XS = carve(2056, KT, T)
    RW.lb = carve(4104, D)
    RW.KS = [carve(4104 + 512 * i, 2, T) for i in range(2)]
    RW.LTl = carve(4104, 8, P)
    RW.g_lb = carve(5128, D)
    RW.w0 = carve(6152, D)
    RW.IP = carve(6152, KT, CH, P)
    RW.V = carve(6152, KT, T)
    RW.D = carve(8200, KT, T)
    RW.K = carve(8200, KT, T)
    RW.sq = carve(10248, KT, T)
    RW.A = carve(10248, KT, T)
    RW.LD = carve(12296, CH, D)
    RW.R = carve(12296, KT, T)
    RW.rB = carve(14344, T)
    RW.PC = carve(14344, KT, CH, P + 1)
    RW.HG = carve(16408, T)
    RW.HW = over_hid[:, 7 * T:8 * T]
    RW.a = over_hid[:, :].rearrange("p (a b) -> p a b", b=T)
    RW.omm, RW.omka, RW.kk1k = carve(16664, 48), carve(16712, 8), carve(16720, 8)
    RW.pz, RW.stats, RW.mv, RW.rs = (carve(16728, 8), carve(16736, 8, 6), carve(16784, 8, 2), carve(16800, 8, 1))
    part = lambda o, n: over_act[:, o:o + n * P].rearrange("p (a b) -> p a b", b=P)
    RW.LT, RW.W, RW.WT, RW.X = (part(1024 * i, 8) for i in range(4))
    RW.AK, RW.RK, RW.RB = carve(0, 8, P), carve(1024, 8, P), carve(14344, 8, P)
    RW.RHS, RW.SA = carve(15368, 8, RN), carve(15880, 8, RN)
    RW.tok = part(1024, 4)
    RW.Z = part(3072, 2)
    RW.vtok = RW.XS.rearrange("p a b -> p (a b)").rearrange("p (m n) -> p m n", m=CH)
    MIXES = [3, 4, 5, 1, 0, 2]
    CUM_BANKS = [6, 7, 2, 3, 4, 5, 6, 7]
    C_DECAY = float(np.exp(-0.5))

    lora_in = sem("lora_in")
    h_ready, d_ready, xs_part, xs_done = (sem(n) for n in (
        "rwkv_input", "token_difference", "mix_part", "mixed"))
    lora_ps, lora_h = sem("lora_in_psum"), sem("lora_hidden")
    yw_ps, yw_sum, ld_done = sem("decay_in_psum"), sem("decay_sum"), sem("decay_sigmoid")
    cum_ps, cum_done = sem("decay_cumulated_in_psum"), sem("decay_exp")
    ag_ps, ag_done = sem("gate_a_in_psum"), sem("gate_a")
    k_taken, r_taken, v_taken = sem("keys_taken"), sem("receptance_taken"), sem("values_taken")
    ks_done, kn_ps, kn_max, kn_done = (sem(n) for n in (
        "key_squares", "key_norms_in_psum", "key_norms_guarded", "key_norm_scales"))
    key_done, scaled = sem("keys_done"), sem("inverse_decayed")
    vt_ps, vt_done = sem("values_by_token_in_psum"), sem("values_by_token")
    bon, bon_ps, bon_done = sem("bonus_products"), sem("bonus_in_psum"), sem("bonus")
    rec_ps, rec_sb = sem("recurrence_in_psum"), sem("recurrence_taken")
    pair_ps = sem("l_in_psum")
    tok_done, gn_done = sem("keys_by_token"), sem("group_norm_scales")
    PE_STEPS = ["AK0", "AK1", "RK0", "RK1", "RB0", "RB1", "RHS0", "SA0", "TOK", "Z", "RHS1", "SA1", "Y", "YT"]
    SB_STEPS = ["AK0", "AK1", "RK0", "RK1", "RB0", "RB1", "RHS0", "SA0", "Z", "RHS1", "SA1", "STATS", "YN", "OUT"]
    ps_at = lambda q, name: len(PE_STEPS) * q + PE_STEPS.index(name) + 1
    sb_at = lambda q, name: len(SB_STEPS) * q + SB_STEPS.index(name) + 1
    block = ctx.enter_context(nc.Block())

    @block.sync
    def _(sp):
        def load(u, s, srcs, i=None, i_step=0):
            if i is None:
                if u >= RING:
                    sp.wait_ge(lo_done, u - RING + 1)
            else:
                sp.wait_ge(lo_done, i * i_step + (u - RING + 1))
            for dst, src in srcs:
                sp.dma_start(dst, src).then_inc(landed[s], 16)

        def inner(u, view, c):
            s = u % RING
            load(u, s, [(raw[s][:, :].rearrange("p (k n) -> p k n", k=KT), view[:, :, c * 256:c * 256 + 256])])

        def outer(u, view, k):
            s = u % RING
            load(u, s, [(two(raw[s][:, :]), view[:, k:k + 2, :])])

        def mlp(j, after_loop=lambda: None):
            up, down = ffn_v[j]
            u0 = FFN_U[j]
            inner(u0, up, 0)
            inner(u0 + 1, up, 1)
            with sp.Fori(0, FCH - 1) as i:
                for q in range(4):
                    u = u0 + 2 + q
                    s = u % RING
                    if q < 2:
                        load(u, s, [(raw[s][:, :].rearrange("p (k n) -> p k n", k=KT),
                                     up[:, :, bass.ds(i * 512 + (512 + q * 256), 256)])], i, 4)
                    else:
                        load(u, s, [(two(raw[s][:, :]), down[:, bass.ds(i * 4 + (q - 2) * 2, 2), :])], i, 4)
            after_loop()
            outer(u0 + 4 * FCH - 2, down, 4 * FCH - 4)
            outer(u0 + 4 * FCH - 1, down, 4 * FCH - 2)

        def load_sgu():
            sp.wait_ge(x_done, X_MIX + 4)
            for dst, src in ((SG.ws[:], dram["w_s_t"]), (SG.bv[:], every(dram["sgu_b_in_2"][0:1, SGU_E:])),
                             (SG.T[:].rearrange("p a b -> p (a b)"), every(dram["sgu_b_s_2"].rearrange("a g i -> a (g i)")))):
                sp.dma_start(dst, src).then_inc(sgu_in, 16)

        def load_lora():
            for dst, src in ((RW.lb[0:64, :], dram["rwkv_w_lora_b_2"][0]), (RW.lb[64:P, :], dram["rwkv_a_lora_b_2"][0]),
                             (RW.g_lb[:], dram["rwkv_g_lora_b_2"][0]), (RW.w0[:], every(dram["rwkv_w0_2"][0:1, :]))):
                sp.dma_start(dst, src).then_inc(lora_in, 16)

        for h in range(2):
            sp.dma_start(x[:, 4 * h:4 * h + 4, :],
                         dram["x_t"].rearrange("(k p) t -> p k t", p=P)[:, 4 * h:4 * h + 4, :]).then_inc(x_in, 16)
        for j, c in enumerate(IN_COLS):
            inner(U_IN + j, w_in_v, c)
            if j == 0:
                sp.dma_start(cm[:], dram["constants"]).then_inc(cm_in, 16)
        for c in range(4):
            inner(U_OUT + c, w_out_v, c)
        if on["ffn1"]:
            mlp(0, after_loop=load_sgu if on["sgu"] else lambda: None)
        if on["sgu"]:
            for c in range(8):
                inner(U_SGU + c, sgu_in_v, 8 + c)
            for c in range(8):
                inner(U_SGU + 8 + c, sgu_in_v, c)
            for c in range(8):
                outer(U_SGO + c, sgu_out_v, 2 * c)
        if on["ffn2"]:
            mlp(1, after_loop=load_lora if on["rwkv"] else lambda: None)
        if on["rwkv"]:
            s = U_LORA % RING
            v = raw[s][:, :].rearrange("p (k n) -> p k n", k=KT)
            load(U_LORA, s, [(v[:, :, 0:64], by_k(dram["rwkv_w_lora_a_2"][0])),
                             (v[:, :, 64:128], by_k(dram["rwkv_a_lora_a_2"][0])),
                             (v[:, :, 128:256], by_k(dram["rwkv_g_lora_a_2"][0]))])
            for q in range(3):
                for c in range(4):
                    inner(U_RKV + 4 * q + c, rkv_v[(1, 0, 2)[q]], c)
            for c in range(4):
                inner(U_WO + c, wo_v, c)
        if on["end"]:
            mlp(2)

        n_out = {"mixer": X_MIX, "ffn1": X_FFN1, "sgu": X_SGU, "ffn2": X_FFN2, "rwkv": X_RWKV,
                 "end": X_FFN3 + 4}[last_phase]
        for c in range(4):
            sp.wait_ge(x_done, n_out + c + 1)
            sp.dma_start(out.rearrange("(k p) t -> p k t", p=P)[:, 2 * c:2 * c + 2, :],
                         x[:, 2 * c:2 * c + 2, :]).then_inc(stored, 16)
        sp.wait_ge(stored, 64)

    @block.gpsimd
    def _(pool):
        chain = Chain(pool, pool_chain)
        chain.add(pool.memset(MX.pre[:, :, 0:3], 0.0))
        pool.wait_ge(cm_in, 16)
        pool.wait_ge(decay_done, 2)
        pool.tensor_tensor(MX.AT[:], MX.ET[:], cmat("upper").rearrange("p (a b) -> p a b", a=1)
                           .broadcast_to([P, 8, P]), ALU.mult).then_inc(decay_mask, 1)
        pool.wait_ge(decay_mask, 1)
        pool.tensor_tensor(MX.ET[:], MX.ET[:], over(cmat("neg_upper_strict"), 8), ALU.mult)\
            .then_inc(decay_mask, 1)

        def inversion(call, LT, LTl):
            pool.wait_ge(lt_ready, 2 * call + 2)
            for l in range(1, LEVELS):
                n = 12 * call + 2 * (l - 1)
                if n:
                    pool.wait_ge(inv_x_ps, n)
                pool.tensor_tensor(LTl[:], LT[:], over(cmat("levels", l), 8), ALU.mult).then_inc(inv_lt, 1)

        pool.wait_ge(proj_out, 8)
        pool.wait_ge(kqn_done, 4)
        for g in range(NPOOL):
            src = MX.pu[:, g, :]
            for d in range(g + 1):
                w = 1 << d
                lo = 2 * w - 1
                chain.settle()
                if d < g:
                    dst = MX.doubling[d % 2]
                    chain.add(pool.tensor_tensor(dst[:, lo:], src[:, lo:], src[:, lo - w:T + 16 - w], ALU.add))
                    src = dst
                else:
                    pool.tensor_tensor(MX.box[:, g, :], src[:, 16:], src[:, 16 - w:T + 16 - w], ALU.add)\
                        .then_inc(box_sum, 1)
                    pool.wait_ge(box_sum, g + 1)
        inversion(0, MX.LT, MX.LTl)
        pool.memset(f32(zeros[:]), 0.0).then_inc(zero_done, 1)
        if on["sgu"]:
            pool.wait_ge(zero_done, 1)
            pool.wait_ge(sgu_in, 48)
            pool.memset(SG.ws[64:P, :, 0:64], 0.0).then_inc(mask_done, 1)
        if on["rwkv"]:
            for k in range(KT):
                pool.wait_ge(h_ready, k + 1)
                pool.tensor_tensor(RW.D[:, k, :], RW.H[:, k, 0:T], RW.H[:, k, 1:T + 1], ALU.subtract).then_inc(d_ready, 1)

            def mixed_low(q):
                for k in range(KT):
                    pool.wait_ge(a_hi, A_RWKV + 8 * q + k + 1)
                    pool.wait_ge(xs_done, 8 * q + k + 1)
                    pool.tensor_tensor(act_lo[:, k, :], RW.XS[:, k, :], f32(act_hi[:, k, :]), ALU.subtract)\
                        .then_inc(a_lo, 1)

            for q in range(1, 5):
                mixed_low(q)
            for c in range(4):
                if c == 2:
                    mixed_low(5)
                pool.wait_ge(key_done, c + 1)
                for dst in (RW.A, RW.K):
                    v = dst[:, 2 * c:2 * c + 2, :].rearrange("p a (m b) -> p a m b", m=CH)
                    pool.tensor_tensor(v, v, RW.IP[:, 2 * c:2 * c + 2, :, :], ALU.mult).then_inc(scaled, 1)
            for q in range(4):
                inversion(1 + q, RW.LT, RW.LTl)

    @block.scalar
    def _(act):
        chain = Chain(act, act_chain)

        def high(u, i=None):
            s = u % RING
            if type(i) is int:
                u, i = u + 4 * i, None
            if i is None:
                act.wait_ge(landed[s], landed_value(u))
                if u >= RING:
                    act.wait_ge(w_used, u - RING + 1)
            else:
                act.wait_ge(landed[s], i * 16 + landed_value(u))
                act.wait_ge(w_used, i * 4 + (u - RING + 1))
            nc.scalar.activation(whi[s][:], raw[s][:], ACT.Copy).then_inc(hi_done, 1)

        def rsqrt_of_sums(dst, ps, n, eps=EPS):
            chain.add(nc.scalar.activation(dst, ps, ACT.Ln, scale=1.0 / n, bias=eps_col(eps)))
            chain.settle()
            return nc.scalar.activation(dst, dst, ACT.Exp, scale=-0.5)

        def eps_col(e):
            return {EPS: epst[:, 0:1], GN_EPS: epst[:, 1:2], LN_EPS: epst[:, 2:3]}[e]

        act.dma_start(vec[:], dram["vectors"]).then_inc(vec_in, 16)
        act.dma_start(MX.wab[:], by_k(dram["w_in"][0])[:, :, IN_WIDTH - 8:IN_WIDTH]).then_inc(ab_in, 16)
        log_exp = lambda: nc.scalar.preload_act_table_set("natural_log_exp_and_others")
        log_exp()
        act.dma_start(MX.wpool[:], dram["w_pool"][0].rearrange("g c d -> c g d")).then_inc(wpool_in, 16)

        act.wait_ge(vec_in, 16)
        act.wait_ge(x_in, 32)
        for k in range(KT):
            nc.scalar.activation(act_hi[:, k, :], x[:, k, :], ACT.Copy, scale=vcol("norm_mix", k)).then_inc(a_hi, 1)
        nc.scalar.activation(MX.sq[:], x[:], ACT.Square).then_inc(sq_done, 1)
        act.wait_ge(ab_in, 16)
        nc.scalar.activation(wab_hi[:], MX.wab[:], ACT.Copy).then_inc(ab_col, 1)
        high(0)
        act.wait_ge(ss_done, 1)
        act.wait_ge(ab_col, 3)
        rsqrt_of_sums(MX.rB, bank[7][:, 0:T], D).then_inc(r_done, 1)
        high(1)
        s = MX.s
        act.wait_ge(ab_col, 4)
        chain.add(nc.scalar.activation(s[2], s[0], ACT.Abs))
        chain.add(nc.scalar.activation(s[5], s[1], ACT.Exp, scale=-1.0))
        chain.add(nc.scalar.activation(s[4][:, 0, :], vcol("a_log", 0, 4), ACT.Exp))
        chain.settle()
        chain.add(nc.scalar.activation(s[2], s[2], ACT.Exp, scale=-1.0))
        chain.settle()
        nc.scalar.activation(s[3], s[2], ACT.Ln, bias=1.0).then_inc(ab_col, 1)
        high(2)
        for m in range(CH):
            act.wait_ge(gsum_ps, m + 1)
            nc.scalar.activation(MX.ET[:, 4 * m:4 * m + 4, :], bank[2 + m][:].rearrange("p (a b) -> p a b", a=4),
                                 ACT.Exp).then_inc(decay_done, 1)
        act.wait_ge(gsum_ps, 3)
        nc.scalar.activation(MX.qg[:], bank[4][:].rearrange("p (a b) -> p a b", a=4), ACT.Exp).then_inc(decay_done, 1)
        nc.scalar.activation(s[8].rearrange("p a b -> p (a b)"), bank[6][:, 20:28], ACT.Exp).then_inc(decay_done, 1)

        for j in range(6):
            high(j + 3)
            act.wait_ge(proj_out, j + 1)
            for t in (2 * j, 2 * j + 1):
                nc.scalar.activation(MX.qkv[:, t, :], MX.pre[:, t, 3:T + 3], ACT.Copy, scale=tap_weight(t, 0))\
                    .then_inc(conv_first, 1)
            act.wait_ge(conv_done, 2 * j + 2)
            nc.scalar.activation(MX.qkv[:, 2 * j:2 * j + 2, :], MX.qkv[:, 2 * j:2 * j + 2, :], ACT.Silu)\
                .then_inc(silu_done, 1)
            if j < 4:
                act.wait_ge(silu_done, j + 1)
                nc.scalar.activation(MX.sq[:, 2 * j:2 * j + 2, :], MX.qkv[:, 2 * j:2 * j + 2, :], ACT.Square)\
                    .then_inc(sq_done, 1)
        log_exp()
        high(9)
        for j in range(4):
            act.wait_ge(ss_done, 2 + j)
            rsqrt_of_sums(MX.sq[:, 2 * j:2 * j + 2, :], two(bank[2 + j][:]), 1.0).then_inc(r_done, 1)
        high(10)
        high(11)
        for m in range(CH):
            act.wait_ge(tr_ps, m + 1)
            nc.scalar.activation(MX.Vt[:, 4 * m:4 * m + 4, :], bank[6 + m][:].rearrange("p (a b) -> p a b", a=4),
                                 ACT.Copy).then_inc(tr_done, 1)
        high(12)
        act.wait_ge(z_done, 2)
        nc.scalar.activation(MX.z[:], MX.z[:], ACT.Silu).then_inc(z_done, 1)
        log_exp()
        for g in range(NPOOL):
            act.wait_ge(pool_ps, g // 2 + 1)
            if g == 0:
                act.wait_ge(w_used, 10)
            nc.scalar.activation(act_hi[:, g, :], two(bank[g // 2][:])[:, g % 2, :], ACT.Copy,
                                 scale=vcol("pool_scale", g)).then_inc(a_hi, 1)
        high(13)

        def inversion(call, W, X):
            for l in range(LEVELS):
                for h in range(2):
                    n = 12 * call + 2 * (l - 1) + h
                    if l:
                        act.wait_ge(inv_x_ps, n + 1)
                        if n >= 2:
                            act.wait_ge(inv_d_ps, n - 1)
                        nc.scalar.activation(X[:, 4 * h:4 * h + 4, :],
                                             bank[h][:].rearrange("p (a b) -> p a b", a=4), ACT.Copy)\
                            .then_inc(inv_x, 1)
                if l < LEVELS - 1:
                    for h in range(2):
                        act.wait_ge(inv_t_ps, 12 * call + 2 * l + h + 1)
                        nc.scalar.activation(W[:, 4 * h:4 * h + 4, :],
                                             bank[4 + h][:].rearrange("p (a b) -> p a b", a=4), ACT.Copy)\
                            .then_inc(inv_w, 1)

        inversion(0, MX.W, MX.X)
        act.wait_ge(step_ps, 2)
        nc.scalar.activation(MX.S[:], bank[7][:].rearrange("p (a b) -> p a b", a=4), ACT.Copy).then_inc(step_sb, 1)
        for h in range(2):
            act.wait_ge(step_ps, 5 + h)
            nc.scalar.activation(MX.R[:].rearrange("p (a c) b -> p a (c b)", a=4)[:, 2 * h:2 * h + 2, :],
                                 two(bank[h][:]), ACT.Square).then_inc(sq_done, 1)
        for h in range(2):
            act.wait_ge(ss_done, 6 + h)
            rsqrt_of_sums(MX.rko[:, 2 * h:2 * h + 2, :], two(bank[2 + h][:]), P).then_inc(r_done, 1)
        for h in range(NGDN):
            act.wait_ge(step_sb, 5 + h)
            nc.scalar.activation(act_hi[:, 4 + h, :], MX.mix[:, h, :], ACT.Copy).then_inc(a_hi, 1)

        if on["ffn1"]:
            high(U_OUT + 4)
            high(U_OUT + 5)

        def mlp(j):
            u0, xd, h0 = FFN_U[j], FFN_X[j], FFN_H[j]
            for k in range(KT):
                act.wait_ge(x_done, xd + k // 2 + 1)
                if k == 0:
                    act.wait_ge(w_used, u0)
                nc.scalar.activation(act_hi[:, k, :], x[:, k, :], ACT.Copy, scale=vcol(FFN_G[j], k)).then_inc(a_hi, 1)
            high(u0 + 2)
            nc.scalar.activation(FB.sq[:], x[:], ACT.Square).then_inc(sq_done, 1)
            high(u0 + 3)

            def relu(i, s):
                act.wait_ge(w_used, i * 4 + (u0 - 2 + s + 1))
                act.wait_ge(h_lo, i * 2 + (h0 - 2 + s + 1))
                nc.scalar.activation(FB.r[:, 2 * s:2 * s + 2, :], two(bank[s][:]), ACT.Relu).then_inc(relu_done, 1)

            def square(i, s):
                act.wait_ge(relu_done, i * 2 + (16 * j + s + 1))
                if not (type(i) is int and i == 0):
                    act.wait_ge(w_used, i * 4 + (u0 + s + 1))
                nc.scalar.activation(hid_hi[:, 2 * s:2 * s + 2, :], FB.r[:, 2 * s:2 * s + 2, :], ACT.Square)\
                    .then_inc(h_hi, 1)

            for s in range(2):
                act.wait_ge(w_used, u0 + s + 1)
                nc.scalar.activation(FB.r[:, 2 * s:2 * s + 2, :], two(bank[s][:]), ACT.Relu).then_inc(relu_done, 1)
            high(u0 + 4)
            high(u0 + 5)

            def body(i, last=False):
                for s in range(2):
                    square(i, s)
                high(u0 + 6, i)
                high(u0 + 7, i)
                for s in range(2):
                    relu(i + 1, s)
                if not last:
                    high(u0 + 8, i)
                    high(u0 + 9, i)

            def body_end(s):
                square(FCH - 1, s)
                if u0 + 4 * FCH < n_units:
                    high(u0 + 4 * FCH + s)

            body(0)
            with act.Fori(1, FCH - 2) as i:
                body(i)
            body(FCH - 2, last=True)
            for s in range(2):
                body_end(s)

        if on["ffn1"]:
            mlp(0)
        if on["sgu"]:
            for c in range(4):
                act.wait_ge(x_done, X_FFN1 + c + 1)
                cs = slice(2 * c, 2 * c + 2)
                nc.scalar.activation(SG.sq[0][:, cs, :], x[:, cs, :], ACT.Square).then_inc(sq_done, 1)
                nc.scalar.activation(SG.sq[1][:, 2 * c, :], x[:, 2 * c, :], ACT.Square, scale=vcol("norm_final", 2 * c))
                nc.scalar.activation(SG.sq[1][:, 2 * c + 1, :], x[:, 2 * c + 1, :], ACT.Square,
                                     scale=vcol("norm_final", 2 * c + 1)).then_inc(sq_done, 1)
            act.wait_ge(ss_done, SS["sgu"] + 1)
            rsqrt_of_sums(SG.r[0], bank[6][:, 0:T], D).then_inc(r_done, 1)
            act.wait_ge(norm_done, 1)
            rsqrt_of_sums(SG.r[1], SG.r[1], D).then_inc(r_done, 1)
            for k in range(KT):
                act.wait_ge(norm_done, 2 + k)
                nc.scalar.activation(act_hi[:, k, :], SG.h[:, k, :], ACT.Copy).then_inc(a_hi, 1)
            high(U_SGU + 2)
            high(U_SGU + 3)
            for c in range(8):
                act.wait_ge(v_raw, c + 1)
                vs = SG.V[:, :, c * 256:c * 256 + 256]
                nc.scalar.activation(vs, vs, ACT.Gelu).then_inc(v_act, 1)
                high(U_SGU + 4 + c)
            log_exp()
            act.wait_ge(v_stat, 1)
            rsqrt_of_sums(SG.rs, SG.mv[:, :, 1:2], 1.0, LN_EPS).then_inc(v_stat, 1)

            def gated_high(q):
                act.wait_ge(y_done, q + 1)
                if q >= 2:
                    act.wait_ge(w_used, U_SGO + q - 1)
                s = q % 2
                nc.scalar.activation(hid_hi[:, 2 * s:2 * s + 2, :], SG.y[s][:], ACT.Copy).then_inc(h_hi, 1)

            for c in range(8):
                if c == 6:
                    gated_high(0)
                act.wait_ge(w_used, U_SGU + 8 + c + 1)
                for t in range(2):
                    nc.scalar.activation(SG.U[:, 2 * c + t, :], two(bank[c % 2][:])[:, t, :], ACT.Gelu,
                                         bias=vcol("b_in_u", 2 * c + t)).then_inc(u_act, 1)
                high(U_SGU + 12 + c)
            log_exp()
            for q in range(1, 8):
                gated_high(q)
                if q <= 4 or (q <= 6 and on["ffn2"]):
                    high(U_SGO + 3 + q)
        if on["ffn2"]:
            mlp(1)
        if on["rwkv"]:
            for c in range(4):
                act.wait_ge(x_done, X_FFN2 + c + 1)
                nc.scalar.activation(RW.sq[:, 2 * c:2 * c + 2, :], x[:, 2 * c:2 * c + 2, :], ACT.Square).then_inc(sq_done, 1)
            act.wait_ge(ss_done, SS["rwkv"] + 1)
            rsqrt_of_sums(RW.rB, bank[6][:, 0:T], D).then_inc(r_done, 1)

            def mixed_high(q):
                if q in (1, 2):
                    act.wait_ge(lora_ps, q)
                elif q:
                    act.wait_ge(w_used, U_RKV + 4 * (q - 3))
                for k in range(KT):
                    act.wait_ge(xs_done, 8 * q + k + 1)
                    nc.scalar.activation(act_hi[:, k, :], RW.XS[:, k, :], ACT.Copy).then_inc(a_hi, 1)

            def mix_part(q):
                for k in range(KT):
                    act.wait_ge(a_lo, A_RWKV + 8 * (q - 1) + k + 1)
                    p = 8 * MIXES[q] + k
                    nc.scalar.activation(RW.XS[:, k, :], RW.H[:, k, 1:T + 1], ACT.Copy, scale=RW.omm[:, p:p + 1])\
                        .then_inc(xs_part, 1)

            def take_keys(c):
                act.wait_ge(w_used, U_RKV + c + 1)
                nc.scalar.activation(RW.K[:, 2 * c:2 * c + 2, :], two(bank[c % 2][:]), ACT.Copy).then_inc(k_taken, 1)

            def key_squares(c):
                if c >= 2:
                    act.wait_ge(key_done, c - 1)
                act.wait_ge(k_taken, c + 1)
                for t in range(2):
                    k = 2 * c + t
                    last = nc.scalar.activation(RW.KS[c % 2][:, t, :], RW.K[:, k, :], ACT.Square, scale=vcol("k_k", k))
                last.then_inc(ks_done, 1)

            def key_scales(c):
                act.wait_ge(kn_max, c + 1)
                ks = RW.KS[c % 2]
                chain.add(nc.scalar.activation(ks, ks, ACT.Ln, scale=2.0 ** 20))
                chain.settle()
                nc.scalar.activation(ks, ks, ACT.Exp, scale=-0.5).then_inc(kn_done, 1)

            nc.scalar.preload_act_table_set("sigmoid_and_others")
            mixed_high(0)
            mixed_high(1)
            act.wait_ge(lora_ps, 1)
            nc.scalar.activation(RW.HW[0:64, :], bank[0][0:64, 0:T], ACT.Tanh).then_inc(lora_h, 1)
            high(U_LORA + 2)
            mixed_high(2)
            nc.scalar.activation(RW.HW[64:P, :], bank[1][64:P, 0:T], ACT.Copy).then_inc(lora_h, 1)
            high(U_LORA + 3)
            act.wait_ge(w_used, U_LORA + 1)
            nc.scalar.activation(RW.HG[:], bank[2][:, 0:T], ACT.Sigmoid).then_inc(lora_h, 1)
            mixed_high(3)
            high(U_LORA + 4)
            for n in range(4):
                act.wait_ge(yw_sum, n + 1)
                ld = RW.LD[:, n // 2, (n % 2) * 512:(n % 2) * 512 + 512]
                nc.scalar.activation(ld, ld, ACT.Sigmoid).then_inc(ld_done, 1)
            take_keys(0)
            high(U_LORA + 5)
            take_keys(1)
            high(U_LORA + 6)
            for c in range(4):
                act.wait_ge(ag_ps, c + 1)
                for t in range(2):
                    k = 2 * c + t
                    last = nc.scalar.activation(RW.A[:, k, :], two(bank[2 + c][:])[:, t, :], ACT.Sigmoid,
                                                bias=vcol("a0", k))
                last.then_inc(ag_done, 1)
            mix_part(4)
            take_keys(2)
            high(U_LORA + 7)
            for k in range(KT):
                act.wait_ge(cum_ps, k + 1)
                ps = bank[CUM_BANKS[k]][:, 0:2 * (P + 1)].rearrange("p (m t) -> p m t", m=CH)
                nc.scalar.activation(RW.PC[:, k, :, :], ps, ACT.Exp, scale=-C_DECAY)
                nc.scalar.activation(RW.IP[:, k, :, :], ps[:, :, 1:P + 1], ACT.Exp, scale=C_DECAY).then_inc(cum_done, 1)
            log_exp()
            mixed_high(4)
            take_keys(3)
            high(U_LORA + 8)
            key_squares(0)
            key_squares(1)
            high(U_LORA + 9)
            key_scales(0)
            mix_part(5)
            high(U_LORA + 10)
            key_scales(1)
            key_squares(2)
            high(U_LORA + 11)
            key_squares(3)
            key_scales(2)
            mixed_high(5)
            high(U_LORA + 12)
            key_scales(3)
            for c in range(5):
                if c < 4:
                    act.wait_ge(w_used, U_RKV + 8 + c + 1)
                    act.wait_ge(scaled, 2 * c + 2)
                    nc.scalar.activation(RW.V[:, 2 * c:2 * c + 2, :], two(bank[c % 2][:]), ACT.Copy).then_inc(v_taken, 1)
                if c:
                    act.wait_ge(vt_ps, c)
                    nc.scalar.activation(RW.vtok[:, :, (c - 1) * 256:c * 256], two(bank[1 + c][:]), ACT.Copy)\
                        .then_inc(vt_done, 1)
                if c < 4:
                    high(U_WO + c)

            for q in range(4):
                inversion(1 + q, RW.W, RW.X)
                act.wait_ge(rec_ps, ps_at(q, "TOK"))
                nc.scalar.activation(RW.tok, bank[2][:].rearrange("p (a b) -> p a b", a=4), ACT.Copy).then_inc(tok_done, 1)
                act.wait_ge(rec_sb, sb_at(q, "STATS"))
                rsqrt_of_sums(RW.rs, RW.mv[:, :, 1:2], 1.0, GN_EPS).then_inc(gn_done, 1)
            for k in range(KT):
                act.wait_ge(rec_sb, sb_at(3, "OUT"))
                nc.scalar.activation(act_hi[:, k, :], RW.R[:, k, :], ACT.Copy).then_inc(a_hi, 1)
            if on["end"]:
                high(U_FFN3)
                high(U_FFN3 + 1)
        if on["end"]:
            mlp(2)
            for c in range(4):
                act.wait_ge(x_done, X_FFN3 + c + 1)
                nc.scalar.activation(FB.sq[:, 2 * c:2 * c + 2, :], x[:, 2 * c:2 * c + 2, :], ACT.Square).then_inc(sq_done, 1)
            act.wait_ge(ss_done, SS["final"] + 1)
            rsqrt_of_sums(FB.r2, bank[6][:, 0:T], D).then_inc(r_done, 1)

    @block.vector
    def _(dve):
        chain = Chain(dve, dve_chain)

        def low(u, i=None):
            s = u % RING
            dve.wait_ge(hi_done, u + 1 if i is None else i * 4 + (u + 1))
            nc.vector.tensor_tensor(wlo[s][:], raw[s][:], f32(whi[s][:]), ALU.subtract).then_inc(lo_done, 1)

        chain.add(nc.vector.memset(epst[:, 0:1], EPS))
        chain.add(nc.vector.memset(epst[:, 1:2], GN_EPS))
        chain.add(nc.vector.memset(epst[:, 2:3], LN_EPS))
        dve.wait_ge(vec_in, 16)
        dve.wait_ge(x_in, 32)
        for k in range(KT):
            dve.wait_ge(a_hi, A_MIX + k + 1)
            nc.vector.scalar_tensor_tensor(act_lo[:, k, :], x[:, k, :], vcol("norm_mix", k), f32(act_hi[:, k, :]),
                                           ALU.mult, ALU.subtract).then_inc(a_lo, 1)
        dve.wait_ge(ab_col, 1)
        nc.vector.tensor_tensor(wab_lo[:], MX.wab[:], f32(wab_hi[:]), ALU.subtract).then_inc(ab_col, 1)
        chain.settle()
        nc.vector.memset(epst[:, 3:4], 1.0).then_inc(ab_col, 1)
        low(0)
        low(1)
        dve.wait_ge(rtok_ps, 1)
        s = MX.s
        chain.add(nc.vector.tensor_copy(s[7][:, 0, 0:2], bank[6][:, 16:18]))
        chain.settle()
        for m in range(CH):
            chain.add(nc.vector.tensor_scalar(MX.ab[:, m, :], bank[6][:, 8 * m:8 * m + 8], s[7][:, 0, m:m + 1], None,
                                              ALU.mult))
        chain.settle()
        for m in range(CH):
            chain.add(nc.vector.tensor_tensor(s[0][:, m, :], MX.ab[:, m, 0:4], vcol("dt_bias", 0, 4), ALU.add))
        chain.add(nc.vector.tensor_copy(s[1], MX.ab[:, :, 4:8]))
        chain.settle()
        nc.vector.tensor_scalar(s[6], s[0], 0.0, None, ALU.max).then_inc(ab_col, 1)
        dve.wait_ge(ab_col, 5)
        chain.add(nc.vector.tensor_tensor(s[6], s[6], s[3], ALU.add))
        chain.add(nc.vector.tensor_scalar(s[5], s[5], 1.0, None, ALU.add))
        chain.settle()
        chain.add(nc.vector.reciprocal(s[5], s[5]))
        for m in range(CH):
            chain.add(nc.vector.scalar_tensor_tensor(s[7][:, m, :], s[6][:, m, :], -1.0, s[4][:, 0, :],
                                                     ALU.mult, ALU.mult))
        chain.settle()
        for m in range(CH):
            for h in range(4):
                nc.vector.tensor_scalar(MX.GS[:, 4 * m + h, :], cmat("lower_strict"), s[7][:, m, h:h + 1], None,
                                        ALU.mult)
        for h in range(4):
            last = nc.vector.tensor_scalar(MX.GO[:, h, :], ones, s[7][:, 1, h:h + 1], None, ALU.mult)
        last.then_inc(g_ready, 1)
        low(2)

        rB2 = over(MX.rB, 2)
        dve.wait_ge(r_done, 1)
        dve.wait_ge(pool_chain, 1)
        for j in range(6):
            dve.wait_ge(w_used, U_IN + j + 1)
            nc.vector.tensor_tensor(MX.pre[:, 2 * j:2 * j + 2, 3:T + 3], two(bank[j % 2][:]), rB2, ALU.mult)\
                .then_inc(proj_out, 1)
            low(j + 3)
            dve.wait_ge(proj_out, j + 1)
            for tap in range(1, CONV):
                for t in (2 * j, 2 * j + 1):
                    if tap == 1:
                        dve.wait_ge(conv_first, t + 1)
                    else:
                        chain.settle(chain.n if tap == CONV - 1 and t % 2 else chain.n - 1)
                    ins = nc.vector.scalar_tensor_tensor(MX.qkv[:, t, :], MX.pre[:, t, 3 - tap:3 - tap + T],
                                                         tap_weight(t, tap), MX.qkv[:, t, :], ALU.mult, ALU.add)
                    if tap < CONV - 1:
                        chain.add(ins)
                    else:
                        ins.then_inc(conv_done, 1)
        low(9)

        def take_pool(j):
            dve.wait_ge(w_used, U_IN + j + 1)
            nc.vector.tensor_tensor(MX.pu[:, 2 * (j - 6):2 * (j - 6) + 2, 16:T + 16], two(bank[j % 2][:]), rB2,
                                    ALU.mult).then_inc(proj_out, 1)

        dve.wait_ge(conv_done, 12)
        nc.vector.memset(MX.pu[:, :, 0:16], 0.0)
        take_pool(6)
        for j in range(4):
            dve.wait_ge(r_done, 2 + j)
            kq = MX.qkv[:, 2 * j:2 * j + 2, :]
            if j < 2:
                nc.vector.tensor_tensor(kq, kq, MX.sq[:, 2 * j:2 * j + 2, :], ALU.mult).then_inc(kqn_done, 1)
            else:
                nc.vector.scalar_tensor_tensor(kq, kq, float(P) ** -0.5, MX.sq[:, 2 * j:2 * j + 2, :], ALU.mult,
                                               ALU.mult).then_inc(kqn_done, 1)
        take_pool(7)
        low(10)
        for j in (8, 9):
            dve.wait_ge(w_used, U_IN + j + 1)
            nc.vector.tensor_tensor(MX.z[:, 2 * (j - 8):2 * (j - 8) + 2, :], two(bank[j % 2][:]), rB2, ALU.mult)\
                .then_inc(z_done, 1)
        low(11)
        dve.wait_ge(proj_out, 8)
        dve.wait_ge(decay_mask, 2)
        for m in range(CH):
            dve.wait_ge(prod_ps, m + 1)
            for h in range(4):
                last = nc.vector.scalar_tensor_tensor(MX.LT[:, 4 * m + h, :], bank[2 + m][:, h * P:h * P + P],
                                                      s[5][:, m, h:h + 1], MX.ET[:, 4 * m + h, :], ALU.mult, ALU.mult)
            last.then_inc(lt_ready, 1)
        for m in range(CH):
            dve.wait_ge(prod_ps, 3 + m)
            at = MX.AT[:, 4 * m:4 * m + 4, :]
            chain.add(nc.vector.tensor_tensor(at, bank[4 + m][:].rearrange("p (a b) -> p a b", a=4), at, ALU.mult))
        def inversion_start(call, LT, WT):
            for h in range(2):
                hs = slice(4 * h, 4 * h + 4)
                dve.wait_ge(lt_ready, 2 * call + h + 1)
                chain.add(nc.vector.tensor_tensor(WT[:, hs, :], LT[:, hs, :], over(cmat("levels", 0), 4), ALU.mult))
                chain.settle()
                nc.vector.tensor_tensor(WT[:, hs, :], WT[:, hs, :], over(ident, 4), ALU.add).then_inc(inv_wt, 1)

        def inversion(call, WT, meanwhile=lambda l: None):
            for l in range(1, LEVELS):
                meanwhile(l)
                for h in range(2):
                    hs = slice(4 * h, 4 * h + 4)
                    dve.wait_ge(inv_d_ps, 12 * call + 2 * (l - 1) + h + 1)
                    dve.wait_ge(inv_wt, 14 * call + 2 * (l - 1) + h + 1)
                    nc.vector.tensor_tensor(WT[:, hs, :], WT[:, hs, :],
                                            bank[2 + h][:].rearrange("p (a b) -> p a b", a=4), ALU.add)\
                        .then_inc(inv_wt, 1)

        inversion_start(0, MX.LT, MX.WT)
        for g in range(NPOOL):
            dve.wait_ge(box_sum, g + 1)
            src, fr = MX.box[:, g, :], MX.pu[:, g, 16:T + 16]
            ph = CMATS["pool_head"][0] + 16 * g
            chain.add(nc.vector.scalar_tensor_tensor(MX.mix[:, g, 16:T], src[:, 16:T], 1.0 / (2 << g), fr[:, 16:T],
                                                     ALU.mult, ALU.subtract))
            chain.add(nc.vector.tensor_tensor(MX.mix[:, g, 0:16], src[:, 0:16], cm[:, ph:ph + 16], ALU.mult))
        for g in range(NPOOL):
            chain.settle(chain.n - 2 * (NPOOL - 1 - g))
            nc.vector.tensor_tensor(MX.mix[:, g, 0:16], MX.mix[:, g, 0:16], MX.pu[:, g, 16:32], ALU.subtract)\
                .then_inc(pool_sum, 1)
        chain.add(nc.vector.tensor_tensor(MX.qg[:], MX.qkv[:, 4:8, P:T], MX.qg[:], ALU.mult))
        dve.wait_ge(tr_ps, 3)
        dve.wait_ge(decay_done, 4)
        for h in range(4):
            (nc.vector.tensor_scalar(MX.Kd[:, h, :], bank[2][:, h * P:h * P + P], s[8][:, 1, h:h + 1], None,
                                              ALU.mult))
        nc.vector.tensor_scalar(s[10][:, 0, :], s[8][:, 0, :], -1.0, None, ALU.mult).then_inc(kqn_done, 1)
        for g in range(NPOOL):
            dve.wait_ge(a_hi, A_OUT + 2 * (g // 2) + 2)
            nc.vector.scalar_tensor_tensor(act_lo[:, g, :], two(bank[g // 2][:])[:, g % 2, :], vcol("pool_scale", g),
                                           f32(act_hi[:, g, :]), ALU.mult, ALU.subtract).then_inc(a_lo, 1)
        low(12)

        inversion(0, MX.WT)
        low(13)
        dve.wait_ge(step_ps, 1)
        for h in range(4):
            last = nc.vector.tensor_scalar(MX.vn[:, h, :], bank[6][:, h * P:h * P + P], s[5][:, 0, h:h + 1], None,
                                           ALU.mult)
        last.then_inc(step_sb, 1)
        dve.wait_ge(step_ps, 3)
        for h in range(4):
            last = nc.vector.scalar_tensor_tensor(MX.R[:, h, :], bank[6][:, h * P:h * P + P], s[10][:, 0, h:h + 1],
                                                  MX.Vt[:, 4 + h, :], ALU.mult, ALU.add)
        last.then_inc(step_sb, 1)
        dve.wait_ge(step_ps, 4)
        for h in range(4):
            last = nc.vector.tensor_scalar(MX.vn[:, 4 + h, :], bank[7][:, h * P:h * P + P], s[5][:, 1, h:h + 1],
                                           None, ALU.mult)
        last.then_inc(step_sb, 1)
        dve.wait_ge(sq_done, 7)
        dve.wait_ge(z_done, 3)
        for h in range(4):
            dve.wait_ge(r_done, 6 + h // 2)
            chain.add(nc.vector.scalar_tensor_tensor(MX.mix[:, h, :], two(bank[h // 2][:])[:, h % 2, :],
                                                     vcol("gdn_norm"), MX.rko[:, h, :], ALU.mult, ALU.mult))
            chain.settle()
            nc.vector.tensor_tensor(MX.mix[:, h, :], MX.mix[:, h, :], MX.z[:, h, :], ALU.mult).then_inc(step_sb, 1)
        for h in range(NGDN):
            dve.wait_ge(a_hi, A_OUT + 4 + h + 1)
            nc.vector.tensor_tensor(act_lo[:, 4 + h, :], MX.mix[:, h, :], f32(act_hi[:, 4 + h, :]), ALU.subtract)\
                .then_inc(a_lo, 1)

        def residual(n0, banks, done, count):
            for c in range(4):
                dve.wait_ge(done, count + c + 1)
                xs = x[:, 2 * c:2 * c + 2, :]
                nc.vector.tensor_tensor(xs, xs, two(bank[banks[c]][:]), ALU.add).then_inc(x_done, 1)

        if on["ffn1"]:
            low(U_OUT + 4)
            low(U_OUT + 5)
        residual(X_MIX, (4, 5, 6, 7), w_used, U_OUT)
        def mlp(j):
            u0, h0 = FFN_U[j], FFN_H[j]
            for k in range(KT):
                dve.wait_ge(a_hi, FFN_A[j] + k + 1)
                nc.vector.scalar_tensor_tensor(act_lo[:, k, :], x[:, k, :], vcol(FFN_G[j], k), f32(act_hi[:, k, :]),
                                               ALU.mult, ALU.subtract).then_inc(a_lo, 1)
            low(u0 + 2)
            low(u0 + 3)
            dve.wait_ge(ss_done, SS[("ffn1", "ffn2", "ffn3")[j]] + 1)
            chain.add(nc.vector.tensor_scalar(FB.r2, bank[6][:, 0:T], 1.0 / D, EPS, ALU.mult, ALU.add))
            chain.settle()
            chain.add(nc.vector.reciprocal(FB.r2, FB.r2))
            low(u0 + 4)
            low(u0 + 5)

            def hidden(i, then=lambda s: None):
                for s in range(2):
                    hs = slice(2 * s, 2 * s + 2)
                    dve.wait_ge(relu_done, i * 2 + (16 * j + s + 1))
                    nc.vector.tensor_tensor(FB.h[:, hs, :], FB.r[:, hs, :], FB.r[:, hs, :], ALU.mult).then_inc(r_sq, 1)
                for s in range(2):
                    hs = slice(2 * s, 2 * s + 2)
                    dve.wait_ge(h_hi, i * 2 + (h0 + s + 1))
                    dve.wait_ge(r_sq, i * 2 + (16 * j + s + 1))
                    nc.vector.tensor_tensor(hid_lo[:, hs, :], FB.h[:, hs, :], f32(hid_hi[:, hs, :]), ALU.subtract)\
                        .then_inc(h_lo, 1)
                    then(s)

            def body(i, last):
                hidden(i)
                low(u0 + 6, i)
                low(u0 + 7, i)
                if not last:
                    low(u0 + 8, i)
                    low(u0 + 9, i)

            with dve.Fori(0, FCH - 2) as i:
                body(i, False)
            body(FCH - 2, True)
            hidden(FCH - 1, lambda s: low(u0 + 4 * FCH + s) if u0 + 4 * FCH < n_units else None)
            chain.settle()
            for c in range(4):
                accumulated(FFN_ACC[j], c, u0 + 4 * FCH)
                t = FB.t[c % 2]
                if c >= 2:
                    dve.wait_ge(x_done, FFN_XO[j] + c - 1)
                chain.add(nc.vector.tensor_tensor(t, two(bank[2 + c][:]), over(FB.r2, 2), ALU.mult))
                chain.settle()
                xs = x[:, 2 * c:2 * c + 2, :]
                nc.vector.tensor_tensor(xs, xs, t, ALU.add).then_inc(x_done, 1)

        def accumulated(a0, c, u_end):
            if c < 3:
                dve.wait_ge(acc_ps, a0 + c + 1)
            else:
                dve.wait_ge(w_used, u_end)

        if on["ffn1"]:
            mlp(0)
        if on["sgu"]:
            dve.wait_ge(sgu_in, 48)
            for q in range(4):
                dve.wait_ge(rs_ps, q + 1)
                for g in range(4 * q, 4 * q + 4):
                    last = nc.vector.scalar_tensor_tensor(SG.T[:, g, :], bank[(0, 1)[q % 2]][:, (g % 4) * P:(g % 4) * P + P],
                                                          vcol("sgu_ln_b", g), SG.T[:, g, :], ALU.mult, ALU.add)
                last.then_inc(t_done, 1)
            dve.wait_ge(r_done, RD["sgu"] + 1)
            dve.wait_ge(ss_done, SS["sgu"] + 2)
            r1, r2 = SG.r
            chain.add(nc.vector.tensor_tensor(r2, r1, r1, ALU.mult))
            chain.settle()
            nc.vector.tensor_tensor(r2, r2, bank[7][:, 0:T], ALU.mult).then_inc(norm_done, 1)
            for k in range(KT):
                ins = nc.vector.scalar_tensor_tensor(x[:, k, :], x[:, k, :], vcol("norm_final", k), r1, ALU.mult,
                                                     ALU.mult)
                if k % 2:
                    ins.then_inc(x_done, 1)
            dve.wait_ge(r_done, RD["sgu"] + 2)

            def normalised_low(k):
                dve.wait_ge(a_hi, A_SGU + k + 1)
                dve.wait_ge(norm_done, 2 + k)
                nc.vector.tensor_tensor(act_lo[:, k, :], SG.h[:, k, :], f32(act_hi[:, k, :]), ALU.subtract)\
                    .then_inc(a_lo, 1)

            for k in range(KT):
                dve.wait_ge(x_done, X_FIN + k // 2 + 1)
                nc.vector.scalar_tensor_tensor(SG.h[:, k, :], x[:, k, :], vcol("norm_mix_g0", k), r2, ALU.mult, ALU.mult)\
                    .then_inc(norm_done, 1)
                if k > 1:
                    normalised_low(k - 2)
            normalised_low(KT - 2)
            normalised_low(KT - 1)
            low(U_SGU + 2)
            low(U_SGU + 3)

            def statistics(c):
                dve.wait_ge(v_act, 2 * c + 2)
                for m in range(CH):
                    n = chain.add(nc.vector.bn_stats(SG.stats[:, m, c, :], SG.V[:, m, c * 512:c * 512 + 512]))

            for c in range(8):
                dve.wait_ge(w_used, U_SGU + c + 1)
                cs = slice(c * 256, c * 256 + 256)
                nc.vector.tensor_tensor(SG.V[:, :, cs], two(bank[c % 2][:]), over(SG.bv[:, cs], 2), ALU.add)\
                    .then_inc(v_raw, 1)
                low(U_SGU + 4 + c)
                if c % 2 and c > 1:
                    statistics(c // 2 - 1)
            statistics(3)
            chain.settle()
            for m in range(CH):
                last = nc.vector.bn_aggr(SG.mv[:, m, :], SG.stats[:, m, :, :].rearrange("p a b -> p (a b)"))
            last.then_inc(v_stat, 1)
            dve.wait_ge(v_stat, 2)
            for m in range(CH):
                nc.vector.tensor_scalar(SG.V[:, m, :], SG.V[:, m, :], SG.mv[:, m, 0:1], SG.rs[:, m, :], ALU.subtract,
                                        ALU.mult).then_inc(vn_done, 1)
            def gate(q):
                s = q % 2
                dve.wait_ge(sp_ps, q + 1)
                if q >= 2:
                    dve.wait_ge(h_hi, H_SGU + q - 1)
                for t in range(2):
                    g = 2 * q + t
                    chain.add(nc.vector.scalar_tensor_tensor(
                        two(SG.y[s][:, t, :]), two(two(bank[6 + s][:])[:, t, :]), vcol("sgu_ln_g", g),
                        over(SG.T[:, g, :], 2), ALU.mult, ALU.add))
                chain.settle()
                dve.wait_ge(u_act, 2 * q + 2)
                nc.vector.tensor_tensor(SG.y[s][:], SG.y[s][:], SG.U[:, 2 * q:2 * q + 2, :], ALU.mult).then_inc(y_done, 1)

                dve.wait_ge(h_hi, H_SGU + q + 1)
                dve.wait_ge(y_done, q + 1)
                nc.vector.tensor_tensor(hid_lo[:, 2 * s:2 * s + 2, :], SG.y[s][:], f32(hid_hi[:, 2 * s:2 * s + 2, :]),
                                        ALU.subtract).then_inc(h_lo, 1)

            dve.wait_ge(t_done, 4)
            for c in range(8):
                low(U_SGU + 12 + c)
                if c == 5:
                    gate(0)
            for q in range(1, 8):
                gate(q)
                if q <= 4 or (q <= 6 and on["ffn2"]):
                    low(U_SGO + 3 + q)
            for c in range(4):
                accumulated(ACC_SGU, c, U_FFN2)
                xs = x[:, 2 * c:2 * c + 2, :]
                nc.vector.tensor_tensor(xs, xs, two(bank[2 + c][:]), ALU.add).then_inc(x_done, 1)
        if on["ffn2"]:
            mlp(1)
        if on["rwkv"]:
            nc.vector.tensor_scalar(RW.omm, vcol("mu", 0, 48), -1.0, 1.0, ALU.mult, ALU.add)
            nc.vector.tensor_scalar(RW.omka, vcol("k_a", 0, 8), -1.0, 1.0, ALU.mult, ALU.add)
            nc.vector.tensor_scalar(RW.kk1k, vcol("k_k", 0, 8), 1024.0, None, ALU.mult)
            chain.add(nc.vector.memset(RW.H[:, :, 0:1], 0.0))
            dve.wait_ge(r_done, RD["rwkv"] + 1)

            def mix(q, k):
                mu = vcol("mu", 8 * MIXES[q] + k)
                if q < 4:
                    dve.wait_ge(d_ready, k + 1)
                    dve.wait_ge(h_ready, k + 1)
                    if q:
                        dve.wait_ge(a_lo, A_RWKV + 8 * (q - 1) + k + 1)
                    nc.vector.scalar_tensor_tensor(RW.XS[:, k, :], RW.D[:, k, :], mu, RW.H[:, k, 1:T + 1], ALU.mult,
                                                   ALU.add).then_inc(xs_done, 1)
                else:
                    dve.wait_ge(xs_part, 8 * (q - 4) + k + 1)
                    nc.vector.scalar_tensor_tensor(RW.XS[:, k, :], RW.H[:, k, 0:T], mu, RW.XS[:, k, :], ALU.mult,
                                                   ALU.add).then_inc(xs_done, 1)

            by_chunk = lambda t: t.rearrange("p a (m b) -> p a m b", m=CH)

            def take_receptance(c):
                dve.wait_ge(w_used, U_RKV + 4 + c + 1)
                dve.wait_ge(cum_done, 8)
                nc.vector.tensor_tensor(by_chunk(RW.R[:, 2 * c:2 * c + 2, :]), by_chunk(two(bank[c % 2][:])),
                                        RW.PC[:, 2 * c:2 * c + 2, :, 1:P + 1], ALU.mult).then_inc(r_taken, 1)

            def guard(c):
                dve.wait_ge(kn_ps, c + 1)
                nc.vector.tensor_scalar(RW.KS[c % 2], two(bank[6 + c % 2][:]), 1e-24, None, ALU.max).then_inc(kn_max, 1)

            def keys(c):
                ks, cs = RW.KS[c % 2], slice(2 * c, 2 * c + 2)
                dve.wait_ge(kn_done, c + 1)
                dve.wait_ge(ag_done, 4)
                for t in range(2):
                    k = 2 * c + t
                    n = chain.add(nc.vector.scalar_tensor_tensor(RW.a[:, k, :], RW.K[:, k, :], RW.kk1k[:, k:k + 1],
                                                                 ks[:, t, :], ALU.mult, ALU.mult))
                chain.settle()
                for t in range(2):
                    k = 2 * c + t
                    chain.add(nc.vector.tensor_scalar(ks[:, t, :], RW.A[:, k, :], vcol("k_a", k), RW.omka[:, k:k + 1],
                                                      ALU.mult, ALU.add))
                chain.settle()
                chain.add(nc.vector.tensor_tensor(RW.A[:, cs, :], RW.A[:, cs, :], RW.a[:, cs, :], ALU.mult))
                nc.vector.tensor_tensor(RW.K[:, cs, :], RW.K[:, cs, :], ks, ALU.mult).then_inc(key_done, 1)
                chain.settle()
                av = by_chunk(RW.a[:, cs, :])
                chain.add(nc.vector.scalar_tensor_tensor(av, av, -1.0, RW.PC[:, cs, :, 0:P], ALU.mult, ALU.mult))

            def bonus_products(c):
                dve.wait_ge(scaled, 2 * c + 2)
                dve.wait_ge(r_taken, c + 1)
                if c >= 2:
                    dve.wait_ge(bon_ps, c - 1)
                else:
                    dve.wait_ge(key_done, c + 3)
                for t in range(2):
                    k = 2 * c + t
                    last = nc.vector.scalar_tensor_tensor(RW.KS[c % 2][:, t, :], RW.R[:, k, :], vcol("r_k", k),
                                                          RW.K[:, k, :], ALU.mult, ALU.mult)
                last.then_inc(bon, 1)

            def bonus(c):
                dve.wait_ge(bon_ps, c + 1)
                dve.wait_ge(vt_ps, c + 1)
                v = RW.V[:, 2 * c:2 * c + 2, :]
                nc.vector.tensor_tensor(v, v, two(bank[6 + c % 2][:]), ALU.mult).then_inc(bon_done, 1)

            for i in range(KT + 3):
                if i < KT:
                    nc.vector.scalar_tensor_tensor(RW.H[:, i, 1:T + 1], x[:, i, :], vcol("norm_mix_g1", i), RW.rB,
                                                   ALU.mult, ALU.mult).then_inc(h_ready, 1)
                if 0 <= i - 2 < KT:
                    mix(0, i - 2)
                k = i - 3
                if k >= 0:
                    dve.wait_ge(a_hi, A_RWKV + k + 1)
                    dve.wait_ge(xs_done, k + 1)
                    nc.vector.tensor_tensor(act_lo[:, k, :], RW.XS[:, k, :], f32(act_hi[:, k, :]), ALU.subtract)\
                        .then_inc(a_lo, 1)
            for q in range(1, 4):
                for k in range(KT):
                    mix(q, k)
                low(U_LORA + 1 + q)
            dve.wait_ge(lora_in, 64)
            for n in range(4):
                dve.wait_ge(yw_ps, n + 1)
                cs = slice((n % 2) * 512, (n % 2) * 512 + 512)
                nc.vector.tensor_tensor(RW.LD[:, n // 2, cs], bank[2 + n][:], RW.w0[:, cs], ALU.add).then_inc(yw_sum, 1)
            low(U_LORA + 5)
            low(U_LORA + 6)
            for k in range(KT):
                mix(4, k)
            low(U_LORA + 7)
            low(U_LORA + 8)
            dve.wait_ge(cum_done, 8)
            chain.add(nc.vector.reciprocal(RW.pz, RW.PC[:, :, 1, 0]))
            chain.settle()
            chain.add(nc.vector.tensor_tensor(RW.pz, RW.pz, RW.PC[:, :, 0, P], ALU.mult))
            take_receptance(0)
            guard(0)
            low(U_LORA + 9)
            keys(0)
            take_receptance(1)
            guard(1)
            for k in range(KT):
                mix(5, k)
            low(U_LORA + 10)
            keys(1)
            take_receptance(2)
            guard(2)
            low(U_LORA + 11)
            keys(2)
            take_receptance(3)
            guard(3)
            low(U_LORA + 12)
            keys(3)
            bonus_products(0)
            bonus_products(1)
            low(U_WO)
            bonus_products(2)
            bonus_products(3)
            for c in range(4):
                bonus(c)
                if c < 3:
                    low(U_WO + 1 + c)
            chain.settle()

            four = lambda ap: ap.rearrange("p (a b) -> p a b", a=4)

            def masked(q, name, dst, mask):
                for m in range(CH):
                    dve.wait_ge(rec_ps, ps_at(q, name + str(m)))
                    nc.vector.tensor_tensor(dst[:, 4 * m:4 * m + 4, :], four(bank[6 + m][:]), over(cmat(mask), 4),
                                            ALU.mult).then_inc(rec_sb, 1)

            def taken(q, name, dst, src):
                dve.wait_ge(rec_ps, ps_at(q, name))
                nc.vector.tensor_copy(dst, src).then_inc(rec_sb, 1)

            def take_l(q):
                for h in range(2):
                    dve.wait_ge(pair_ps, 2 * q + h + 1)
                    nc.vector.tensor_tensor(RW.LT[:, 4 * h:4 * h + 4, :], four(bank[6 + h][:]),
                                            over(cmat("upper_strict"), 4), ALU.mult).then_inc(lt_ready, 1)

            dve.wait_ge(w_used, U_WO)
            take_l(0)
            inversion_start(1, RW.LT, RW.WT)
            for q in range(4):
                def meanwhile(l):
                    if l == 1:
                        masked(q, "AK", RW.AK, "upper_strict")
                    elif l == 2:
                        masked(q, "RK", RW.RK, "upper")
                    elif l == 3:
                        masked(q, "RB", RW.RB, "upper")
                    elif l == 4:
                        taken(q, "RHS0", RW.RHS[:, 0:4, :], four(bank[6][:, 0:T]))

                inversion(1 + q, RW.WT, meanwhile)
                taken(q, "SA0", RW.SA[:, 0:4, :], four(bank[7][:, 0:T]))
                dve.wait_ge(rec_ps, ps_at(q, "Z"))
                for t in range(2):
                    last = nc.vector.scalar_tensor_tensor(RW.Z[:, t, :], bank[6][:, t * P:t * P + P],
                                                          RW.pz[:, 2 * q + t:2 * q + t + 1], cmat("heads"), ALU.mult,
                                                          ALU.mult)
                last.then_inc(rec_sb, 1)
                taken(q, "RHS1", RW.RHS[:, 4:8, :], four(bank[4][:, 0:T]))
                taken(q, "SA1", RW.SA[:, 4:8, :], four(bank[5][:, 0:T]))
                dve.wait_ge(rec_ps, ps_at(q, "Y"))
                y = bank[0][:].rearrange("p (a b) -> p a b", a=8)
                for n in range(8):
                    chain.add(nc.vector.bn_stats(RW.stats[:, n, :], y[:, n, :]))
                chain.settle()
                for n in range(8):
                    last = nc.vector.bn_aggr(RW.mv[:, n, :], RW.stats[:, n, :])
                last.then_inc(rec_sb, 1)
                if q < 3:
                    dve.wait_ge(inv_lt, 6 * (2 + q))
                    take_l(q + 1)
                dve.wait_ge(gn_done, q + 1)
                for n in range(8):
                    last = nc.vector.tensor_scalar(RW.RHS[:, n, :], y[:, n, :], RW.mv[:, n, 0:1], RW.rs[:, n, :],
                                                   ALU.subtract, ALU.mult)
                last.then_inc(rec_sb, 1)
                if q < 3:
                    inversion_start(2 + q, RW.LT, RW.WT)
                dve.wait_ge(rec_ps, ps_at(q, "YT"))
                cs = slice(2 * q, 2 * q + 2)
                for t in range(2):
                    k = 2 * q + t
                    chain.add(nc.vector.tensor_scalar(RW.R[:, k, :], two(bank[1][:])[:, t, :], vcol("rwkv_ln_g", k),
                                                      vcol("rwkv_ln_b", k), ALU.mult, ALU.add))
                chain.settle()
                chain.add(nc.vector.tensor_tensor(RW.R[:, cs, :], RW.R[:, cs, :], RW.V[:, cs, :], ALU.add))
                chain.settle()
                nc.vector.tensor_tensor(RW.R[:, cs, :], RW.R[:, cs, :], two(bank[3][:]), ALU.mult).then_inc(rec_sb, 1)
            for k in range(KT):
                dve.wait_ge(a_hi, A_WO + k + 1)
                nc.vector.tensor_tensor(act_lo[:, k, :], RW.R[:, k, :], f32(act_hi[:, k, :]), ALU.subtract)\
                    .then_inc(a_lo, 1)
            if on["end"]:
                low(U_FFN3)
                low(U_FFN3 + 1)
            residual(X_RWKV, (4, 5, 6, 7), w_used, U_WO)
        if on["end"]:
            mlp(2)
            dve.wait_ge(r_done, RD["final"] + 1)
            for k in range(KT):
                ins = nc.vector.scalar_tensor_tensor(x[:, k, :], x[:, k, :], vcol("final_norm_g", k), FB.r2, ALU.mult,
                                                     ALU.mult)
                if k % 2:
                    ins.then_inc(x_done, 1)

    @block.tensor
    def _(pe):
        def split_matmul(dst, l_hi, l_lo, r_hi, r_lo, start, stop, **kw):
            nc.tensor.matmul(dst, l_lo, r_hi, start=start, stop=False, **kw)
            nc.tensor.matmul(dst, l_hi, r_lo, start=False, stop=False, **kw)
            return nc.tensor.matmul(dst, l_hi, r_hi, start=False, stop=stop, **kw)

        def project(u, b, a0=None):
            s = u % RING
            h, l = (w[s][:, :].rearrange("p (k n) -> p k n", k=KT) for w in (whi, wlo))
            pe.wait_ge(lo_done, u + 1)
            for t in range(2):
                for k in range(KT):
                    if t == 0 and a0 is not None:
                        pe.wait_ge(a_lo, a0 + k + 1)
                    cs = slice(t * P, t * P + P)
                    last = split_matmul(bank[b][:, t * T:t * T + T], h[:, k, cs], l[:, k, cs], act_hi[:, k, :],
                                        act_lo[:, k, :], start=k == 0, stop=k == KT - 1)
            last.then_inc(w_used, 1)
            return last

        def sum_squares(sq, n, dst):
            for k in range(n):
                last = nc.tensor.matmul(dst, ones, sq[:, k, :], start=k == 0, stop=k == n - 1)
            return last

        pe.wait_ge(cm_in, 16)
        pe.wait_ge(sq_done, 1)
        sum_squares(MX.sq, KT, bank[7][:, 0:T]).then_inc(ss_done, 1)
        pe.wait_ge(ab_col, 2)
        pe.wait_ge(a_lo, KT)
        for m in range(CH):
            for k in range(KT):
                ms = slice(m * P, m * P + P)
                split_matmul(bank[6][:, 8 * m:8 * m + 8], act_hi[:, k, ms], act_lo[:, k, ms], wab_hi[:, k, :],
                             wab_lo[:, k, :], start=k == 0, stop=k == KT - 1)

        def take(j):
            if j >= 2:
                pe.wait_ge(proj_out, j - 1)
            project(U_IN + j, j % 2)

        take(0)
        pe.wait_ge(r_done, 1)
        for m in range(CH):
            last = nc.tensor.matmul(bank[6][:, 16 + m:17 + m], MX.rB[0:1, m * P:m * P + P], ones[0:1, 0:1],
                                    start=True, stop=True)
        last.then_inc(rtok_ps, 1)
        take(1)
        pe.wait_ge(g_ready, 1)
        for m in range(CH):
            for h in range(4):
                last = nc.tensor.matmul(bank[2 + m][:, h * P:h * P + P], MX.GS[:, 4 * m + h, :], cmat("upper"),
                                        start=True, stop=True)
            last.then_inc(gsum_ps, 1)
        for h in range(4):
            nc.tensor.matmul(bank[4][:, h * P:h * P + P], MX.GO[:, h, :], cmat("upper"), start=True, stop=True)
        nc.tensor.matmul(bank[6][:, 20:24], cmat("upper"), MX.s[7][:, 1, :], start=True, stop=True)
        nc.tensor.matmul(bank[6][:, 24:28], cmat("lower_strict"), MX.s[7][:, 0, :], start=True, stop=True)\
            .then_inc(gsum_ps, 1)
        for j in range(2, 6):
            take(j)
        pe.wait_ge(decay_done, 4)
        for j in range(2):
            pe.wait_ge(sq_done, 2 + j)
            for t in range(2):
                last = nc.tensor.matmul(bank[2 + j][:, t * T:t * T + T], ones, MX.sq[:, 2 * j + t, :], start=True,
                                        stop=True)
            last.then_inc(ss_done, 1)
        take(6)
        for j in range(2, 4):
            pe.wait_ge(sq_done, 2 + j)
            for t in range(2):
                last = nc.tensor.matmul(bank[2 + j][:, t * T:t * T + T], ones, MX.sq[:, 2 * j + t, :], start=True,
                                        stop=True)
            last.then_inc(ss_done, 1)
        take(7)
        pe.wait_ge(silu_done, 6)
        for m in range(CH):
            for h in range(4):
                last = nc.tensor.transpose(bank[6 + m][:, h * P:h * P + P], MX.qkv[:, 8 + h, m * P:m * P + P], ident)
            last.then_inc(tr_ps, 1)
        take(8)
        pe.wait_ge(kqn_done, 4)
        for q in range(2):
            for m in range(CH):
                for h in range(4):
                    ms = slice(m * P, m * P + P)
                    last = nc.tensor.matmul(bank[2 + 2 * q + m][:, h * P:h * P + P], MX.qkv[:, h, ms],
                                            MX.qkv[:, 4 * q + h, ms], start=True, stop=True)
                last.then_inc(prod_ps, 1)
        take(9)
        pe.wait_ge(lt_ready, 1)
        for h in range(4):
            last = nc.tensor.transpose(bank[2][:, h * P:h * P + P], MX.qkv[:, h, 0:P], ident)
        last.then_inc(tr_ps, 1)
        pe.wait_ge(wpool_in, 16)
        pe.wait_ge(z_done, 2)
        for g in range(NPOOL):
            pe.wait_ge(pool_sum, g + 1)
            last = nc.tensor.matmul(bank[g // 2][:, (g % 2) * T:(g % 2) * T + T], MX.wpool[:, g, :], MX.mix[:, g, :],
                                    start=True, stop=True)
            if g % 2:
                last.then_inc(pool_ps, 1)

        def inversion(call, W, WT, X, LTl, between=lambda l: None):
            for l in range(LEVELS):
                if l:
                    between(l)
                    pe.wait_ge(inv_lt, 6 * call + l)
                    for h in range(2):
                        pe.wait_ge(inv_w, 12 * call + 2 * (l - 1) + h + 1)
                        n = 12 * call + 2 * (l - 1) + h
                        if n >= 2:
                            pe.wait_ge(inv_x, n - 1)
                        for q in range(4):
                            last = nc.tensor.matmul(bank[h][:, q * P:q * P + P], LTl[:, 4 * h + q, :], W[:, 4 * h + q, :],
                                                    start=True, stop=True)
                        last.then_inc(inv_x_ps, 1)
                    for h in range(2):
                        pe.wait_ge(inv_x, 12 * call + 2 * (l - 1) + h + 1)
                        for q in range(4):
                            last = nc.tensor.matmul(bank[2 + h][:, q * P:q * P + P], X[:, 4 * h + q, :],
                                                    WT[:, 4 * h + q, :], start=True, stop=True)
                        last.then_inc(inv_d_ps, 1)
                if l < LEVELS - 1:
                    for h in range(2):
                        pe.wait_ge(inv_wt, 14 * call + 2 * l + h + 1)
                        if l:
                            pe.wait_ge(inv_w, 12 * call + 2 * (l - 1) + h + 1)
                        for q in range(4):
                            last = nc.tensor.transpose(bank[4 + h][:, q * P:q * P + P], WT[:, 4 * h + q, :], ident)
                        last.then_inc(inv_t_ps, 1)

        def between(l):
            if l == 1:
                pe.wait_ge(a_lo, A_OUT + 4)
                pe.wait_ge(kqn_done, 5)

        inversion(0, MX.W, MX.WT, MX.X, MX.LTl, between)
        pe.wait_ge(inv_wt, 14)
        pe.wait_ge(tr_done, 2)
        hp = lambda h: slice(h * P, h * P + P)
        for h in range(4):
            last = nc.tensor.matmul(bank[6][:, hp(h)], MX.WT[:, h, :], MX.Vt[:, h, :], start=True, stop=True)
        last.then_inc(step_ps, 1)
        pe.wait_ge(step_sb, 1)
        for h in range(4):
            last = nc.tensor.matmul(bank[7][:, hp(h)], MX.Kd[:, h, :], MX.vn[:, h, :], start=True, stop=True)
        last.then_inc(step_ps, 1)
        pe.wait_ge(step_sb, 2)
        for h in range(4):
            last = nc.tensor.matmul(bank[6][:, hp(h)], MX.qkv[:, h, P:T], MX.S[:, h, :], start=True, stop=True)
        last.then_inc(step_ps, 1)
        pe.wait_ge(step_sb, 3)
        for h in range(4):
            last = nc.tensor.matmul(bank[7][:, hp(h)], MX.WT[:, 4 + h, :], MX.R[:, h, :], start=True, stop=True)
        last.then_inc(step_ps, 1)
        for h in range(4):
            b, c = bank[h // 2], (h % 2) * T
            nc.tensor.matmul(b[:, c:c + P], MX.vn[:, h, :], MX.AT[:, h, :], start=True, stop=True)
            nc.tensor.matmul(b[:, c + P:c + T], MX.S[:, h, :], MX.qg[:, h, :], start=True, stop=False)
            if h == 0:
                pe.wait_ge(step_sb, 4)
            last = nc.tensor.matmul(b[:, c + P:c + T], MX.vn[:, 4 + h, :], MX.AT[:, 4 + h, :], start=False, stop=True)
            if h % 2:
                last.then_inc(step_ps, 1)
        Rq = MX.R[:].rearrange("p (a c) b -> p a (c b)", a=4)
        for h in range(2):
            pe.wait_ge(sq_done, 6 + h)
            for t in range(2):
                last = nc.tensor.matmul(bank[2 + h][:, t * T:t * T + T], ones, Rq[:, 2 * h + t, :], start=True, stop=True)
            last.then_inc(ss_done, 1)
        for c in range(4):
            project(U_OUT + c, 4 + c, A_OUT if c == 0 else None)

        def clear_accumulators():
            for b in range(2, 6):
                for t in range(2):
                    nc.tensor.matmul(bank[b][:, t * T:t * T + T], zeros[:, 0:P], zeros[:], start=t == 0, stop=False,
                                     skip_group_check=True)

        def accumulate(u, s, i=None, last=False):
            q = u % RING
            h, l = two(whi[q][:, :]), two(wlo[q][:, :])
            pe.wait_ge(lo_done, u + 1 if i is None else i * 4 + (u + 1))
            for n in range(KT):
                cs = slice(n * P, n * P + P)
                dst = bank[2 + n // 2][:, (n % 2) * T:(n % 2) * T + T]
                for k in range(2):
                    ins = split_matmul(dst, h[:, k, cs], l[:, k, cs], hid_hi[:, 2 * s + k, :], hid_lo[:, 2 * s + k, :],
                                       start=False, stop=last and k == 1, skip_group_check=True)
                if last and n % 2 and n < KT - 1:
                    ins.then_inc(acc_ps, 1)
            ins.then_inc(w_used, 1)

        def mlp(j):
            u0, h0, a0 = FFN_U[j], FFN_H[j], FFN_A[j]

            def up(u, s, i=None, first=False):
                q = u % RING
                h, l = (w[q][:, :].rearrange("p (k n) -> p k n", k=KT) for w in (whi, wlo))
                pe.wait_ge(lo_done, u + 1 if i is None else i * 4 + (u + 1))
                if i is not None:
                    pe.wait_ge(relu_done, i * 2 + (16 * j + s + 1))
                for t in range(2):
                    for k in range(KT):
                        if first and t == 0 and s == 0:
                            pe.wait_ge(a_lo, a0 + k + 1)
                        cs = slice(t * P, t * P + P)
                        ins = split_matmul(bank[s][:, t * T:t * T + T], h[:, k, cs], l[:, k, cs], act_hi[:, k, :],
                                           act_lo[:, k, :], start=k == 0, stop=k == KT - 1)
                ins.then_inc(w_used, 1)

            up(u0, 0, first=True)
            up(u0 + 1, 1)
            pe.wait_ge(sq_done, SQ[("ffn1", "ffn2", "ffn3")[j]] + 1)
            sum_squares(FB.sq, KT, bank[6][:, 0:T]).then_inc(ss_done, 1)
            clear_accumulators()
            with pe.Fori(0, FCH - 1) as i:
                for s in range(2):
                    up(u0 + 2 + s, s, i)
                for s in range(2):
                    pe.wait_ge(h_lo, i * 2 + (h0 + s + 1))
                    accumulate(u0 + 4 + s, s, i)
            for s in range(2):
                pe.wait_ge(h_lo, h0 + 2 * FCH - 2 + s + 1)
                accumulate(u0 + 4 * FCH - 2 + s, s, last=s == 1)

        pe.wait_ge(zero_done, 1)
        if on["ffn1"]:
            mlp(0)
        if on["sgu"]:
            pe.wait_ge(mask_done, 1)
            for q in range(4):
                if q >= 2:
                    pe.wait_ge(t_done, q - 1)
                else:
                    pe.wait_ge(relu_done, 16)
                nc.tensor.matmul(bank[q % 2][:], ones, SG.ws[:, 4 * q:4 * q + 4, :].rearrange("p a b -> p (a b)"),
                                 start=True, stop=True).then_inc(rs_ps, 1)
            for c in range(4):
                for v in range(2):
                    pe.wait_ge(sq_done, SQ["sgu"] + 2 * c + v + 1)
                    for t in range(2):
                        k = 2 * c + t
                        ins = nc.tensor.matmul(bank[6 + v][:, 0:T], ones, SG.sq[v][:, k, :], start=k == 0, stop=k == KT - 1)
                    if c == 3:
                        ins.then_inc(ss_done, 1)
            for c in range(8):
                u = U_SGU + c
                q = u % RING
                h, l = (w[q][:, :].rearrange("p (k n) -> p k n", k=KT) for w in (whi, wlo))
                pe.wait_ge(lo_done, u + 1)
                if c >= 2:
                    pe.wait_ge(v_raw, c - 1)
                else:
                    pe.wait_ge(t_done, 3 + c)
                for m in range(CH):
                    ms = slice(m * P, m * P + P)
                    for k in range(KT):
                        if c == 0 and m == 0:
                            pe.wait_ge(a_lo, A_SGU + k + 1)
                        ins = split_matmul(bank[c % 2][:, m * T:m * T + T], act_hi[:, k, ms], act_lo[:, k, ms], h[:, k, :],
                                           l[:, k, :], start=k == 0, stop=k == KT - 1)
                ins.then_inc(w_used, 1)
            def spatial(q):
                if q >= 2:
                    pe.wait_ge(y_done, q - 1)
                for t in range(2):
                    g = 2 * q + t
                    for m in range(CH):
                        ins = nc.tensor.matmul(bank[6 + q % 2][:, t * T + m * P:t * T + m * P + P],
                                               SG.V[:, m, g * P:g * P + P], SG.ws[:, g, :], start=True, stop=True)
                ins.then_inc(sp_ps, 1)

            for c in range(8):
                if c >= 6:
                    pe.wait_ge(vn_done, 2)
                    spatial(c - 6)
                if c >= 2:
                    pe.wait_ge(u_act, 2 * (c - 1))
                else:
                    pe.wait_ge(v_raw, 7 + c)
                project(U_SGU + 8 + c, c % 2)
            clear_accumulators()
            for q in range(8):
                pe.wait_ge(h_lo, H_SGU + q + 1)
                accumulate(U_SGO + q, q % 2, last=q == 7)
                if q + 2 < 8:
                    spatial(q + 2)
        if on["ffn2"]:
            mlp(1)
        if on["rwkv"]:
            for c in range(4):
                pe.wait_ge(sq_done, SQ["rwkv"] + c + 1)
                for k in (2 * c, 2 * c + 1):
                    ins = nc.tensor.matmul(bank[6][:, 0:T], ones, RW.sq[:, k, :], start=k == 0, stop=k == KT - 1)
            ins.then_inc(ss_done, 1)
            s = U_LORA % RING
            h, l = (w[s][:, :].rearrange("p (k n) -> p k n", k=KT) for w in (whi, wlo))
            pe.wait_ge(lo_done, U_LORA + 1)
            for q in range(3):
                ns = slice(P, 2 * P) if q == 2 else slice(0, P)
                for k in range(KT):
                    pe.wait_ge(a_lo, A_RWKV + 8 * q + k + 1)
                    ins = split_matmul(bank[q][:, 0:T], h[:, k, ns], l[:, k, ns], act_hi[:, k, :], act_lo[:, k, :],
                                       start=k == 0, stop=k == KT - 1)
                ins.then_inc(w_used if q == 2 else lora_ps, 1)

            def unit(n):
                if n < 2:
                    pe.wait_ge(lora_h, n + 1)
                else:
                    pe.wait_ge((k_taken, r_taken, v_taken)[(n - 2) // 4], (n - 2) % 4 + 1)
                project(U_RKV + n, n % 2, A_RWKV + 8 * (3 + n // 4) if n % 4 == 0 else None)

            def key_norms(c):
                pe.wait_ge(ks_done, c + 1)
                pe.wait_ge(cum_done, 8) if c < 2 else pe.wait_ge(kn_max, c - 1)
                for t in range(2):
                    ins = nc.tensor.matmul(bank[6 + c % 2][:, t * T:t * T + T], cmat("heads"), RW.KS[c % 2][:, t, :],
                                           start=True, stop=True)
                ins.then_inc(kn_ps, 1)

            unit(0)
            pe.wait_ge(lora_in, 64)
            pe.wait_ge(lora_h, 3)
            for n in range(4):
                m = n // 2
                nc.tensor.matmul(bank[2 + n][:], RW.HW[0:64, m * P:m * P + P],
                                 RW.lb[0:64, (n % 2) * 512:(n % 2) * 512 + 512], start=True, stop=True).then_inc(yw_ps, 1)
            unit(1)
            for c in range(4):
                pe.wait_ge(yw_sum, c + 1)
                for t in range(2):
                    k = 2 * c + t
                    ins = nc.tensor.matmul(bank[2 + c][:, t * T:t * T + T], RW.lb[64:P, k * P:k * P + P],
                                           RW.HW[64:P, :], start=True, stop=True)
                ins.then_inc(ag_ps, 1)
            unit(2)
            pe.wait_ge(ld_done, 4)
            a, n_cum = CMATS["cum"]
            pe.wait_ge(ag_done, 4)

            def cumulate(k):
                if k >= 6:
                    pe.wait_ge(cum_done, k - 5)
                for m in range(CH):
                    ins = nc.tensor.matmul(bank[CUM_BANKS[k]][:, m * n_cum:m * n_cum + n_cum],
                                           RW.LD[:, m, k * P:k * P + P], cm[:, a:a + n_cum], start=True, stop=True)
                ins.then_inc(cum_ps, 1)

            for k in range(6):
                cumulate(k)
            unit(3)
            cumulate(6)
            cumulate(7)
            for c in range(3):
                unit(4 + c)
                key_norms(c)
            unit(7)

            def values_by_token(c):
                pe.wait_ge(v_taken, c + 1)
                pe.wait_ge(ag_done, c + 1)
                for m in range(CH):
                    for t in range(2):
                        o = m * T + t * P
                        ins = nc.tensor.transpose(bank[2 + c][:, o:o + P], RW.V[:, 2 * c + t, m * P:m * P + P], ident)
                ins.then_inc(vt_ps, 1)

            def bonus_sums(c):
                pe.wait_ge(bon, c + 1)
                if c >= 2:
                    pe.wait_ge(bon_done, c - 1)
                for t in range(2):
                    ins = nc.tensor.matmul(bank[6 + c % 2][:, t * T:t * T + T], cmat("heads"), RW.KS[c % 2][:, t, :],
                                           start=True, stop=True)
                ins.then_inc(bon_ps, 1)

            unit(8)
            key_norms(3)
            unit(9)
            values_by_token(0)
            unit(10)
            bonus_sums(0)
            values_by_token(1)
            bonus_sums(1)
            unit(11)
            for c in (2, 3):
                values_by_token(c)
                bonus_sums(c)

            pe.wait_ge(v_taken, 4)
            pe.wait_ge(vt_done, 4)
            pe.wait_ge(bon_done, 4)
            HEADS = [(t, e) for t in range(2) for e in range(2)]
            mat = lambda m, t, e: 4 * e + 2 * m + t
            for q in range(4):
                def pairs(q, left, right, banks, done):
                    for e in range(2):
                        es = slice(RN * e, RN * e + RN)
                        for m in range(CH):
                            for t in range(2):
                                ms, o = slice(m * P, m * P + P), (2 * m + t) * P
                                ins = nc.tensor.matmul(bank[banks[e]][:, o:o + P], left[es, 2 * q + t, ms],
                                                       right[es, 2 * q + t, ms], start=True, stop=True)
                        ins.then_inc(done, 1)

                def v_of(m, h, n=1):
                    o = 256 * q + RN * h
                    return RW.vtok[:, m, o:o + RN * n]

                def between(l):
                    if l == 1:
                        if q:
                            pe.wait_ge(rec_sb, sb_at(q - 1, "OUT"))
                        pe.wait_ge(lt_ready, 2 * (2 + q))
                        pairs(q, RW.K, RW.a, (6, 7), rec_ps)
                    elif l == 2:
                        pe.wait_ge(rec_sb, sb_at(q, "AK1"))
                        pairs(q, RW.K, RW.R, (6, 7), rec_ps)
                    elif l == 3:
                        pe.wait_ge(rec_sb, sb_at(q, "RK1"))
                        pairs(q, RW.A, RW.R, (6, 7), rec_ps)
                    elif l == 4:
                        pe.wait_ge(rec_sb, sb_at(q, "RB1"))
                        for h, (t, e) in enumerate(HEADS):
                            ins = nc.tensor.matmul(bank[6][:, h * RN:h * RN + RN], RW.AK[:, mat(0, t, e), :], v_of(0, h),
                                                   start=True, stop=True)
                        ins.then_inc(rec_ps, 1)

                if q == 0:
                    pairs(0, RW.A, RW.a, (6, 7), pair_ps)
                inversion(1 + q, RW.W, RW.WT, RW.X, RW.LTl, between)
                pe.wait_ge(inv_wt, 14 * (2 + q))
                pe.wait_ge(rec_sb, sb_at(q, "RHS0"))
                for h, (t, e) in enumerate(HEADS):
                    ins = nc.tensor.matmul(bank[7][:, h * RN:h * RN + RN], RW.WT[:, mat(0, t, e), :], RW.RHS[:, h, :],
                                           start=True, stop=True)
                ins.then_inc(rec_ps, 1)
                for i, src in enumerate((RW.A, RW.K)):
                    for t in range(2):
                        o = (2 * i + t) * P
                        ins = nc.tensor.transpose(bank[2][:, o:o + P], src[:, 2 * q + t, 0:P], ident)
                ins.then_inc(rec_ps, 1)
                pe.wait_ge(tok_done, q + 1)
                pe.wait_ge(rec_sb, sb_at(q, "SA0"))
                for t in range(2):
                    dst = bank[6][:, t * P:t * P + P]
                    nc.tensor.matmul(dst, RW.tok[:, t, :], RW.SA[:, 2 * t:2 * t + 2, :].rearrange("p a b -> p (a b)"),
                                     start=True, stop=False)
                    ins = nc.tensor.matmul(dst, RW.tok[:, 2 + t, :], v_of(0, 2 * t, 2), start=False, stop=True)
                ins.then_inc(rec_ps, 1)
                pe.wait_ge(rec_sb, sb_at(q, "Z"))
                for t in range(2):
                    nc.tensor.matmul(bank[4][:, t * P:t * P + P], RW.a[:, 2 * q + t, P:T], RW.Z[:, t, :], start=True,
                                     stop=True)
                    for e in range(2):
                        h = 2 * t + e
                        ins = nc.tensor.matmul(bank[4][:, h * RN:h * RN + RN], RW.AK[:, mat(1, t, e), :], v_of(1, h),
                                               start=False, stop=True, skip_group_check=True)
                ins.then_inc(rec_ps, 1)
                pe.wait_ge(rec_sb, sb_at(q, "RHS1"))
                for h, (t, e) in enumerate(HEADS):
                    ins = nc.tensor.matmul(bank[5][:, h * RN:h * RN + RN], RW.WT[:, mat(1, t, e), :],
                                           RW.RHS[:, 4 + h, :], start=True, stop=True)
                ins.then_inc(rec_ps, 1)
                for h, (t, e) in enumerate(HEADS):
                    dst, n = bank[0][:, h * RN:h * RN + RN], mat(0, t, e)
                    nc.tensor.matmul(dst, RW.RK[:, n, :], v_of(0, h), start=True, stop=False)
                    nc.tensor.matmul(dst, RW.RB[:, n, :], RW.SA[:, h, :], start=False, stop=True)
                pe.wait_ge(rec_sb, sb_at(q, "SA1"))
                for t in range(2):
                    nc.tensor.matmul(bank[0][:, T + t * P:T + t * P + P], RW.R[:, 2 * q + t, P:T], RW.Z[:, t, :],
                                     start=True, stop=True)
                    for e in range(2):
                        h, n = 2 * t + e, mat(1, t, e)
                        dst = bank[0][:, T + h * RN:T + h * RN + RN]
                        nc.tensor.matmul(dst, RW.RK[:, n, :], v_of(1, h), start=False, stop=False,
                                         skip_group_check=True)
                        ins = nc.tensor.matmul(dst, RW.RB[:, n, :], RW.SA[:, 4 + h, :], start=False, stop=True,
                                               skip_group_check=True)
                ins.then_inc(rec_ps, 1)
                if q < 3:
                    pairs(q + 1, RW.A, RW.a, (6, 7), pair_ps)
                for t in range(2):
                    k = 2 * q + t
                    nc.tensor.matmul(bank[3][:, t * T:t * T + T], RW.g_lb[:, k * P:k * P + P], RW.HG[:], start=True,
                                     stop=True)
                pe.wait_ge(rec_sb, sb_at(q, "YN"))
                for t in range(2):
                    for m in range(CH):
                        o = t * T + m * P
                        src = RW.RHS[:, 4 * m + 2 * t:4 * m + 2 * t + 2, :].rearrange("p a b -> p (a b)")
                        ins = nc.tensor.transpose(bank[1][:, o:o + P], src, ident)
                ins.then_inc(rec_ps, 1)
            for c in range(4):
                project(U_WO + c, 4 + c, A_WO if c == 0 else None)
        if on["end"]:
            mlp(2)
            for c in range(4):
                pe.wait_ge(sq_done, SQ["final"] + c + 1)
                for k in (2 * c, 2 * c + 1):
                    ins = nc.tensor.matmul(bank[6][:, 0:T], ones, FB.sq[:, k, :], start=k == 0, stop=k == KT - 1)
            ins.then_inc(ss_done, 1)


def kernel(**inputs):
    from concourse import bacc
    from concourse.bass_utils import run_bass_kernel_spmd

    a = {k: np.asarray(v) for k, v in inputs.items()}

    def tiles(v):
        return v.reshape(-1, P).T

    conv = a["conv_w"][0]
    conv = conv.T.reshape(12, P, CONV).transpose(1, 0, 2).reshape(P, 12 * CONV)
    one_row = lambda v: np.broadcast_to(v[None, :], (P, v.shape[0]))
    columns = {
        "norm_mix": tiles(a["norm_mix"][0]), "conv_w": conv, "pool_scale": tiles(a["pool_scale"][0]),
        "gdn_norm": tiles(a["gdn_norm"][0]), "norm_mlp": tiles(a["norm_mlp"][0]),
        "norm_final": tiles(a["norm_final"]), "norm_mix_g0": tiles(a["norm_mix_g_2"][0]),
        "norm_ffn_g0": tiles(a["norm_ffn_g_2"][0]), "norm_mix_g1": tiles(a["norm_mix_g_2"][1]),
        "norm_ffn_g1": tiles(a["norm_ffn_g_2"][1]), "final_norm_g": tiles(a["final_norm_g_2"]),
        "b_in_u": tiles(a["sgu_b_in_2"][0][:SGU_E]), "sgu_ln_g": tiles(a["sgu_ln_g_2"][0]),
        "sgu_ln_b": tiles(a["sgu_ln_b_2"][0]), "mu": tiles(a["rwkv_mu_2"][0].reshape(-1)),
        "a0": tiles(a["rwkv_a0_2"][0]), "k_k": tiles(a["rwkv_k_k_2"][0]), "k_a": tiles(a["rwkv_k_a_2"][0]),
        "r_k": tiles(a["rwkv_r_k_2"][0].reshape(-1)), "rwkv_ln_g": tiles(a["rwkv_ln_g_2"][0]),
        "rwkv_ln_b": tiles(a["rwkv_ln_b_2"][0]), "a_log": one_row(a["a_log"][0]),
        "dt_bias": one_row(a["dt_bias"][0]),
    }
    arrays = {
        "x_t": a["x"][0].T,
        "vectors": np.concatenate([columns[n] for n in VECS], 1),
        "constants": constant_matrices(),
        "w_s_t": a["sgu_w_s_2"][0].transpose(2, 0, 1),
    }
    for n in ("w_in", "w_pool", "w_out", "w_up", "w_down", "ffn_w1_2", "ffn_w2_2", "sgu_w_in_2", "sgu_b_in_2",
              "sgu_b_s_2", "sgu_w_out_2", "rwkv_w_rkv_2", "rwkv_w0_2", "rwkv_w_lora_a_2", "rwkv_w_lora_b_2",
              "rwkv_a_lora_a_2", "rwkv_a_lora_b_2", "rwkv_g_lora_a_2", "rwkv_g_lora_b_2", "rwkv_w_o_2"):
        arrays[n] = a[n]
    arrays = {n: np.ascontiguousarray(v) for n, v in arrays.items()}
    nc = bacc.Bacc("TRN2", target_bir_lowering=False, num_devices=1)
    dram = {
        n: nc.dram_tensor("in_" + n, v.shape, mybir.dt.from_np(v.dtype), kind="ExternalInput").ap()
        for n, v in arrays.items()}
    out = nc.dram_tensor("out_t", (D, T), F32, kind="ExternalOutput").ap()
    build_program(nc, dram, out)
    r = run_bass_kernel_spmd(nc, [{"in_" + n: v for n, v in arrays.items()}], core_ids=[0])
    return np.ascontiguousarray(r.results[0]["out_t"].T)[None]
```
